# Optimizing a Trainium2 kernel written in Bass

```python
import functools
import jax, jax.numpy as jnp
from jax import lax
import numpy as np

D_MODEL = 1024
BATCH = 1
SEQ = 512
DEPTH = 2
DEC_BATCH = 1
DEC_SEQ = 32
PAST_LEN = 1024

CHUNK = 64
HEAD_DIM = 64
H_RET = 4
H_GLA = 4
H_ATT = 8
W_RET = H_RET * HEAD_DIM
W_GLA = H_GLA * HEAD_DIM
W_ATT = H_ATT * HEAD_DIM
MIX_WIDTH = W_RET + W_GLA + W_ATT
GLA_RANK = 16
GLA_TAU = 16.0
BAND_CHUNKS = 8
ATT_REACH = BAND_CHUNKS * CHUNK
REL_MAX = 256
N_REL = CHUNK + REL_MAX
D_FF = 4 * D_MODEL
ROPE_BASE = 10000.0
EPS = 1e-6
IN_COLS = 4 * W_RET + 4 * W_GLA + GLA_RANK + 3 * W_ATT

kernel_name = 'hybrid_stream_encoder_step'

def rmsnorm(x, w):
    xf = x.astype(jnp.float32)
    y = xf * lax.rsqrt(jnp.mean(xf * xf, axis=-1, keepdims=True) + EPS)
    return (y * w.astype(jnp.float32)).astype(x.dtype)

def rotary(x, pos):
    half = HEAD_DIM // 2
    inv_freq = ROPE_BASE ** (-jnp.arange(half, dtype=jnp.float32) / half)
    ang = pos.astype(jnp.float32)[:, None] * inv_freq[None, :]
    cos = jnp.cos(ang)[None, :, None, :]
    sin = jnp.sin(ang)[None, :, None, :]
    x1, x2 = x[..., :half], x[..., half:]
    return jnp.concatenate([x1 * cos - x2 * sin, x1 * sin + x2 * cos], axis=-1)

def retention_log_decay():
    return jnp.log1p(-jnp.exp2(-5.0 - jnp.arange(H_RET, dtype=jnp.float32)))

def project(hn, w_in_l, w_a2_l, b_a_l, pos):
    B, L, _ = hn.shape
    proj = (hn @ w_in_l).astype(jnp.float32)
    sizes = (W_RET,) * 4 + (W_GLA,) * 4 + (GLA_RANK,) + (W_ATT,) * 3
    offsets, acc = [], 0
    for s in sizes[:-1]:
        acc += s
        offsets.append(acc)
    qa, ka, va, ga, qb, kb, vb, gb, low, qc, kc, vc = jnp.split(proj, offsets, axis=-1)
    heads = lambda t: t.reshape(B, L, -1, HEAD_DIM)
    scale = HEAD_DIM ** -0.5
    qa = rotary(heads(qa), pos)
    ka = rotary(heads(ka), pos) * scale
    qb = heads(qb) * scale
    log_f = jax.nn.log_sigmoid(low @ w_a2_l.astype(jnp.float32) + b_a_l.astype(jnp.float32)) / GLA_TAU
    return (qa, ka, heads(va), ga, qb, heads(kb), heads(vb), gb, heads(log_f),
            heads(qc), heads(kc), heads(vc))

def retention_chunk(S, q, k, v, log_gamma):
    L = q.shape[1]
    idx = jnp.arange(L)
    diff = idx[:, None] - idx[None, :]
    causal = diff >= 0
    dpos = jnp.where(causal, diff, 0).astype(jnp.float32)
    decay = jnp.where(causal[None], jnp.exp(dpos[None] * log_gamma[:, None, None]), 0.0)
    scores = jnp.einsum('bthd,bshd->bhts', q, k) * decay[None]
    intra = jnp.einsum('bhts,bshv->bthv', scores, v)
    q_decay = jnp.exp((idx + 1).astype(jnp.float32)[:, None] * log_gamma[None, :])
    inter = jnp.einsum('bthd,bhdv->bthv', q, S) * q_decay[None, :, :, None]
    k_decay = jnp.exp((L - 1 - idx).astype(jnp.float32)[:, None] * log_gamma[None, :])
    S_new = (jnp.exp(L * log_gamma)[None, :, None, None] * S
             + jnp.einsum('bshd,bshv->bhdv', k * k_decay[None, :, :, None], v))
    return S_new, intra + inter

def gla_chunk(S, q, k, v, log_f):
    L = q.shape[1]
    idx = jnp.arange(L)
    b = jnp.cumsum(log_f, axis=1)
    mask = (idx[:, None] >= idx[None, :])[None, :, :, None, None]
    diff = b[:, :, None] - b[:, None, :]
    w = jnp.where(mask, jnp.exp(jnp.where(mask, diff, 0.0)), 0.0)
    scores = jnp.sum(q[:, :, None] * k[:, None, :] * w, axis=-1)
    intra = jnp.einsum('btsh,bshv->bthv', scores, v)
    inter = jnp.einsum('bthd,bhdv->bthv', q * jnp.exp(b), S)
    b_last = b[:, -1]
    S_new = (jnp.exp(b_last)[..., None] * S
             + jnp.einsum('bshd,bshv->bhdv', k * jnp.exp(b_last[:, None] - b), v))
    return S_new, intra + inter

def scan_chunks(step, S0, *seqs):
    B, L = seqs[0].shape[:2]
    n = L // CHUNK
    xs = tuple(jnp.moveaxis(t.reshape(B, n, CHUNK, *t.shape[2:]), 1, 0) for t in seqs)
    S, outs = lax.scan(lambda c, xt: step(c, *xt), S0, xs)
    return S, jnp.moveaxis(outs, 0, 1).reshape(B, L, *outs.shape[3:])

def band_attention(q, k, v, q_pos, k_pos, k_valid, rel_bias_l):
    s = jnp.einsum('bnqhd,bnkhd->bhnqk', q, k) * (HEAD_DIM ** -0.5)
    dist = q_pos[:, :, None] - k_pos[:, None, :]
    ridx = jnp.clip(dist, -(CHUNK - 1), REL_MAX) + (CHUNK - 1)
    s = s + rel_bias_l.astype(jnp.float32)[:, ridx][None]
    s = jnp.where(k_valid[None, None, :, None, :], s, -1e30)
    p = jax.nn.softmax(s, axis=-1)
    return jnp.einsum('bhnqk,bnkhd->bnqhd', p, v)

def prompt_band_attention(q, k, v, rel_bias_l):
    B, L, H, d = q.shape
    n = L // CHUNK

    def band(t):
        tp = jnp.pad(t, ((0, 0), (ATT_REACH, 0), (0, 0), (0, 0))).reshape(B, n + BAND_CHUNKS, CHUNK, H, d)
        return jnp.concatenate([tp[:, j:j + n] for j in range(BAND_CHUNKS + 1)], axis=2)

    q_pos = jnp.arange(L).reshape(n, CHUNK)
    k_pos = (jnp.arange(n)[:, None] - BAND_CHUNKS) * CHUNK + jnp.arange((BAND_CHUNKS + 1) * CHUNK)[None, :]
    out = band_attention(q.reshape(B, n, CHUNK, H, d), band(k), band(v), q_pos, k_pos, k_pos >= 0, rel_bias_l)
    return out.reshape(B, L, H, d)

def sample_band_attention(q, k_new, v_new, k_cache, v_cache, rel_bias_l):
    B, L, H, d = q.shape
    R = k_cache.shape[1]
    k_all = jnp.concatenate([k_cache.astype(jnp.float32), k_new], axis=1)[:, None]
    v_all = jnp.concatenate([v_cache.astype(jnp.float32), v_new], axis=1)[:, None]
    q_pos = (PAST_LEN + jnp.arange(L))[None]
    k_pos = jnp.concatenate([PAST_LEN - R + jnp.arange(R), PAST_LEN + jnp.arange(L)])[None]
    out = band_attention(q[:, None], k_all, v_all, q_pos, k_pos, k_pos >= 0, rel_bias_l)
    return out[:, 0]

def merge_heads(oa, ga, ob, gb, oc, gn_w, gla_w, w_out_l, dtype):
    B, L = oa.shape[:2]
    mu = jnp.mean(oa, axis=-1, keepdims=True)
    var = jnp.mean(jnp.square(oa - mu), axis=-1, keepdims=True)
    a = ((oa - mu) * lax.rsqrt(var + EPS)).reshape(B, L, W_RET) * gn_w.astype(jnp.float32) * jax.nn.silu(ga)
    b = (ob * lax.rsqrt(jnp.mean(ob * ob, axis=-1, keepdims=True) + EPS)).reshape(B, L, W_GLA)
    b = b * gla_w.astype(jnp.float32) * jax.nn.silu(gb)
    cat = jnp.concatenate([a, b, oc.reshape(B, L, W_ATT)], axis=-1)
    return (cat.astype(dtype) @ w_out_l).astype(dtype)

def channel_mix(h, n2, w_up_l, w_down_l):
    u = rmsnorm(h, n2) @ w_up_l
    return (jnp.square(jax.nn.relu(u)) @ w_down_l).astype(h.dtype)

def setup_inputs(seed: int = 0) -> dict:
    key = jax.random.key(seed)
    ks = jax.random.split(key, 20)
    f32 = jnp.float32
    nrm = lambda k, shape, s: jax.random.normal(k, shape, f32) * s
    cache_rows = min(ATT_REACH, PAST_LEN)
    return {
        'x_prompt': nrm(ks[0], (BATCH, SEQ, D_MODEL), 1.0),
        'x_sample': nrm(ks[1], (DEC_BATCH, DEC_SEQ, D_MODEL), 1.0),
        'state_ret': nrm(ks[2], (DEPTH, DEC_BATCH, H_RET, HEAD_DIM, HEAD_DIM), 0.5),
        'state_gla': nrm(ks[3], (DEPTH, DEC_BATCH, H_GLA, HEAD_DIM, HEAD_DIM), 0.5),
        'cache_attn_k': nrm(ks[4], (DEPTH, DEC_BATCH, cache_rows, H_ATT, HEAD_DIM), 1.0),
        'cache_attn_v': nrm(ks[5], (DEPTH, DEC_BATCH, cache_rows, H_ATT, HEAD_DIM), 1.0),
        'norm1_w': 1.0 + nrm(ks[6], (DEPTH, D_MODEL), 0.02),
        'norm2_w': 1.0 + nrm(ks[7], (DEPTH, D_MODEL), 0.02),
        'final_norm_w': 1.0 + nrm(ks[8], (D_MODEL,), 0.02),
        'w_in': nrm(ks[9], (DEPTH, D_MODEL, IN_COLS), D_MODEL ** -0.5),
        'w_gla_a2': nrm(ks[10], (DEPTH, GLA_RANK, W_GLA), GLA_RANK ** -0.5),
        'b_gla_a': nrm(ks[11], (DEPTH, W_GLA), 0.1),
        'ret_gn_w': 1.0 + nrm(ks[12], (DEPTH, W_RET), 0.02),
        'gla_norm_w': 1.0 + nrm(ks[13], (DEPTH, W_GLA), 0.02),
        'rel_bias': nrm(ks[14], (DEPTH, H_ATT, N_REL), 0.1),
        'w_out': nrm(ks[15], (DEPTH, MIX_WIDTH, D_MODEL), MIX_WIDTH ** -0.5),
        'w_up': nrm(ks[16], (DEPTH, D_MODEL, D_FF), D_MODEL ** -0.5),
        'w_down': nrm(ks[17], (DEPTH, D_FF, D_MODEL), D_FF ** -0.5),
    }

def reference(x_prompt, x_sample, state_ret, state_gla, cache_attn_k, cache_attn_v,
              norm1_w, norm2_w, final_norm_w, w_in, w_gla_a2, b_gla_a, ret_gn_w,
              gla_norm_w, rel_bias, w_out, w_up, w_down):
    f32 = jnp.float32
    log_gamma = retention_log_decay()
    ret_step = functools.partial(retention_chunk, log_gamma=log_gamma)
    bp, lp = x_prompt.shape[0], x_prompt.shape[1]
    pos_p = jnp.arange(lp)
    pos_s = PAST_LEN + jnp.arange(x_sample.shape[1])
    keep = min(ATT_REACH, lp)
    hp, hs = x_prompt, x_sample
    ret_p, gla_p, kp, vp, ret_s, gla_s, k_s, v_s = [], [], [], [], [], [], [], []
    for l in range(DEPTH):
        qa, ka, va, ga, qb, kb, vb, gb, lf, qc, kc, vc = project(
            rmsnorm(hp, norm1_w[l]), w_in[l], w_gla_a2[l], b_gla_a[l], pos_p)
        Sa, oa = scan_chunks(ret_step, jnp.zeros((bp, H_RET, HEAD_DIM, HEAD_DIM), f32), qa, ka, va)
        Sb, ob = scan_chunks(gla_chunk, jnp.zeros((bp, H_GLA, HEAD_DIM, HEAD_DIM), f32), qb, kb, vb, lf)
        oc = prompt_band_attention(qc, kc, vc, rel_bias[l])
        hp = hp + merge_heads(oa, ga, ob, gb, oc, ret_gn_w[l], gla_norm_w[l], w_out[l], hp.dtype)
        hp = hp + channel_mix(hp, norm2_w[l], w_up[l], w_down[l])
        ret_p.append(Sa)
        gla_p.append(Sb)
        kp.append(kc[:, lp - keep:])
        vp.append(vc[:, lp - keep:])
        qa, ka, va, ga, qb, kb, vb, gb, lf, qc, kc, vc = project(
            rmsnorm(hs, norm1_w[l]), w_in[l], w_gla_a2[l], b_gla_a[l], pos_s)
        Sa, oa = retention_chunk(state_ret[l].astype(f32), qa, ka, va, log_gamma)
        Sb, ob = gla_chunk(state_gla[l].astype(f32), qb, kb, vb, lf)
        oc = sample_band_attention(qc, kc, vc, cache_attn_k[l], cache_attn_v[l], rel_bias[l])
        hs = hs + merge_heads(oa, ga, ob, gb, oc, ret_gn_w[l], gla_norm_w[l], w_out[l], hs.dtype)
        hs = hs + channel_mix(hs, norm2_w[l], w_up[l], w_down[l])
        ret_s.append(Sa)
        gla_s.append(Sb)
        k_s.append(kc)
        v_s.append(vc)
    y_prompt = rmsnorm(hp, final_norm_w)
    y_sample = rmsnorm(hs, final_norm_w)
    return (y_prompt, y_sample, jnp.stack(ret_p), jnp.stack(gla_p), jnp.stack(kp), jnp.stack(vp),
            jnp.stack(ret_s), jnp.stack(gla_s), jnp.stack(k_s), jnp.stack(v_s))


_drawn_inputs = setup_inputs


def setup_inputs(seed=0):
    import zlib

    import numpy as np

    out = dict(_drawn_inputs(seed))
    spreads = {}
    factors = {'final_norm_w': 2.998, 'ret_gn_w': 7.366, 'gla_norm_w': 7.392, 'rel_bias': 5.682}
    for name, (base, spread) in spreads.items():
        noise = np.random.default_rng([zlib.crc32(name.encode()), seed]).standard_normal(out[name].shape)
        drawn = base * np.exp(spread * noise) if base else spread * noise
        out[name] = __import__('jax').numpy.asarray(drawn.astype(out[name].dtype))
    for name, factor in factors.items():
        out[name] = (out[name] * factor).astype(out[name].dtype)
    return out
```

```python
from contextlib import ExitStack

import numpy as np

import concourse.bass as bass
from concourse import mybir

P = 128
D = 1024
KC = D // P
TP, TS = 512, 32
T = TP + TS
HT = T // 2
L = 2
HD = 64
CH = 64
NC = TP // CH
NT = TP // P
FF = 4 * D
GROUPS = FF // D
LEVELS = [32, 16, 8, 4, 2, 1]
EPS = 1e-6
RAW, SPL = 4, 2
N_IN, N_OUT = 28, KC
N_MLP = 2 * KC
UNITS = N_IN + N_OUT + GROUPS * N_MLP
PW = 2 * T
NEG = -1e30
M0 = 4
NSM = 24
ROPE_BASE, PAST = 10000.0, 1024

F32, F32R, U32 = mybir.dt.float32, mybir.dt.float32r, mybir.dt.uint32
ALU, ACT = mybir.AluOpType, mybir.ActivationFunctionType
AX_X = mybir.AxisListType.X
RADD = bass.bass_isa.ReduceOp.add

GK, GQ, GV, RK, RQ, RV, AQ, GATE = 0, 2, 4, 6, 8, 10, 12, 24
GLA, RET = 0, 1
PE_STEPS = {
    (2, 0): [("rms",), ("low",)],
    (3, 1): [("z",)],
    (5, 0): [("diag", GLA)],
    (5, 1): [("level", 0)], (6, 0): [("level", 1)], (6, 1): [("level", 2)],
    (7, 0): [("level", 3)], (7, 1): [("level", 4)], (8, 0): [("level", 5)],
    (8, 1): [("tok", GLA, "v")], (9, 0): [("tok", GLA, "k")], (9, 1): [("kv", GLA)],
    (10, 1): [("out", GLA)], (11, 0): [("out_s", GLA)],
    (11, 1): [("diag", RET)],
    (12, 0): [("tok", RET, "v")], (12, 1): [("tok", RET, "k")], (13, 0): [("kv", RET)],
    (13, 1): [("back", GLA)],
    (14, 0): [("out", RET)], (14, 1): [("out_s", RET)], (15, 1): [("back", RET)],
}
for _u in range(4):
    _b = 16 + 3 * _u
    PE_STEPS[(_b, 0)] = [("pv_s", _u - 1)] * (_u > 0) + [("score", _u, 0)]
    PE_STEPS[(_b, 1)] = [("heads", _u)]
    PE_STEPS[(_b + 1, 0)] = [("score", _u, 1), ("score_s", _u)]
    PE_STEPS[(_b + 1, 1)] = [("turn", _u, 0)]
    PE_STEPS[(_b + 2, 0)] = [("turn", _u, 1)]
    PE_STEPS[(_b + 2, 1)] = [("pv", _u), ("turn_s", _u)]
DVE_STEPS, ACT_STEPS = dict(PE_STEPS), dict(PE_STEPS)
for _steps in (DVE_STEPS, ACT_STEPS):
    _steps[(4, 1)] = [("cum",)]
    _steps[(11, 1)] = _steps[(11, 1)] + [("gn", GLA)]
    _steps[(15, 0)] = [("gn", RET)]
for _slot, _step in (((8, 0), ("rotary", RK, 0)), ((8, 1), ("rotary", RK, 1)),
                     ((10, 0), ("rotary", RQ, 0)), ((10, 1), ("rotary", RQ, 1))):
    DVE_STEPS[_slot] = DVE_STEPS.get(_slot, []) + [_step]
for _u in range(4):
    _b = 16 + 3 * _u
    DVE_STEPS[(_b + 1, 0)] = [("norm", _u, 0), ("score", _u, 1)]
    DVE_STEPS[(_b + 1, 1)] = [("score_s", _u), ("norm", _u, 1)]
    DVE_STEPS[(_b + 2, 0)] = [("norm_s", _u)]
    DVE_STEPS[(_b + 2, 1)] = [("pv", _u)]
    ACT_STEPS[(_b + 1, 0)] = [("score", _u, 1)]
    ACT_STEPS[(_b + 1, 1)] = [("turn", _u, 0), ("score_s", _u)]
SLOTS = [(n, half) for n in range(2, N_IN) for half in range(2)]

P_OFF = [0, 128, 384, 768]
T_OFF = [0, 512, 1024, 896]
P_COLS = 1280


SCORE = [(3, 0, 0), (2, 1, 0), (0, 1, 384), (1, 2, 0)]
TURN_COLS = [(0, 512), (512, 1024), (1024, 1280)]


def f32(ap):
    return ap.bitcast(F32)


def bank(n):
    return M0 + 2 if n == 2 else 2 * (n % 2)


def blocks(t, c0, c1, H):
    return t[:, c0:c1].rearrange("p (b x h) -> p b x h", x=2, h=H)


def level_parts(H):
    if 2 * H > TS:
        return [(g, g * T, g * T + TP) for g in range(2)]
    return [(0, 0, PW)]


def hybrid_encoder(nc, x, wu, w_low, a2, small, wf, bias, bias_s, st_ret, st_gla, ck, cv,
                   cos_t, sin_t, reset, lmask, dmask, qdec, kdec, sdec,
                   y_p, y_s, ret_p, gla_p, k_p, v_p, ret_s, gla_s, k_s, v_s):
    ctx = ExitStack()
    with ctx:
        place = [(nc.sbuf_base + 63) // 64 * 64]

        def at(name, shape, offset, dt=F32):
            return nc.alloc_sbuf_tensor_at(name, shape, dt, offset=offset)

        def sb(name, shape, dt=F32):
            n = int(np.prod(shape[1:])) * 4
            t = at(name, shape, place[0], dt)
            place[0] += (n + 31) // 32 * 32
            return t

        raw = [sb(f"raw{i}", [P, D]) for i in range(RAW)]
        whi = [sb(f"whi{i}", [P, D], F32R) for i in range(SPL)]
        wlo = [sb(f"wlo{i}", [P, D], F32R) for i in range(SPL)]
        h = sb("h", [P, KC, T])
        xhi, xlo = sb("xhi", [P, KC, T], F32R), sb("xlo", [P, KC, T], F32R)
        zone = place[0]
        zhi, zlo = sb("zhi", [P, KC, T], F32R), sb("zlo", [P, KC, T], F32R)
        rstd, r2 = sb("rstd", [P, T]), sb("r2", [P, T])
        sq = [sb(f"sq{i}", [P, T]) for i in range(2)]
        ssum = sb("ssum", [P, T])
        nt = [sb(f"nt{i}", [P, T]) for i in range(2)]
        ident, ones = sb("ident", [P, P]), sb("ones", [P, P])
        cos_sb, sin_sb = sb("cos_sb", [P, T]), sb("sin_sb", [P, T])
        reset_sb = sb("reset_sb", [P, T])
        lm_sb = sb("lm_sb", [P, 6, 32], U32)
        dm_sb = sb("dm_sb", [P, 2, 4, CH])
        qd_sb, kd_sb = sb("qd_sb", [P, 2, CH]), sb("kd_sb", [P, 2, CH + TS])
        sd_sb = sb("sd_sb", [P, 2, 2])
        low_sb = sb("low_sb", [P, KC, 32])
        a2_sb = sb("a2_sb", [P, 256])
        sm = sb("sm", [P, NSM])
        wf_sb = sb("wf_sb", [P, KC])
        dec = sb("dec", [P, 2, NC + 1])
        gst = [sb(f"gst{i}", [P, 20]) for i in range(3)]
        mx, rs = sb("mx", [P, 2, 4]), sb("rs", [P, 2, 4])
        mxs, rss = sb("mxs", [64, 1]), sb("rss", [64, 1])
        qkv = [[sb(f"att_{n}{i}", [P, T]) for n in "qkv"] for i in range(2)]
        arena = place[0]
        Z = 4 * PW
        gk, gq, gv, gb = (at(n, [P, PW], zone + i * Z) for i, n in enumerate(["gk", "gq", "gv", "gb"]))
        F = [at(f"F{i}", [P, PW], zone + (4 + i) * Z) for i in range(2)]
        qe_g = at("qe_g", [P, PW], zone + 6 * Z)
        QK = [at("QK0", [P, PW], zone + 7 * Z), at("QK1", [P, PW], arena)]
        osq = at("osq", [P, 20 * HD], zone + 4 * Z)
        oT = [at(f"oT{j}", [P, T], zone + j * 4 * T) for j in range(4)]
        G = [at(f"G{j}", [P, T], zone + (KC + j) * 4 * T) for j in range(4)]
        rot = [at("rot0", [P, T], arena + Z), at("rot1", [P, T], arena + Z + 4 * T)]
        rv, rk, rq = (at(n, [P, PW], arena + (2 + i) * Z) for i, n in enumerate(["rv", "rk", "rq"]))
        o = arena + 5 * Z
        ktok, vtok = at("ktok", [P, 5, 256], o), at("vtok", [P, 5, 256], o + 5120)
        Pm = at("Pm", [P, 16, CH], o + 10240)
        Ps = at("Ps", [TS, 4, TS], o + 14336)
        S = at("S", [P, 2, NC + 1, HD], o + 14848)
        Ss = at("Ss", [P, 2, 2, HD], o + 19456)
        O = at("O", [P, 20 * HD], o + 20480)
        end1 = o + 25600
        o = arena
        ckb = [at(f"ckb{i}", [P, NT, P], o + 2048 * i) for i in range(2)]
        cvb = [at(f"cvb{i}", [P, NT, P], o + 4096 + 2048 * i) for i in range(2)]
        Bh = [at(f"Bh{i}", [P, TP], o + 8192 + 2048 * i) for i in range(2)]
        o = arena + 3 * Z
        vtk = [at(f"vtk{i}", [P, 5, P], o + 2560 * i) for i in range(2)]
        ktk = [at(f"ktk{i}", [P, 5, P], o + 5120 + 2560 * i) for i in range(2)]
        kct = at("kct", [P, TP], o + 10240)
        Pr = [at(f"Pr{i}", [P, P_COLS], o + 12288 + 5120 * i) for i in range(2)]
        PT = [at(f"PT{i}", [P, P_COLS], o + 22528 + 5120 * i) for i in range(2)]
        PTs = at("PTs", [P, 5, 64], o + 32768)
        end2 = o + 32768 + 1280
        assert max(end1, end2) <= nc.sbuf_usable_end, (end1, end2, nc.sbuf_usable_end)
        Prs = at("Prs", [64, T], end2)
        Bs = at("Bs", [64, T], zone + (2 * KC - 1) * 4 * T)
        assert end2 + 2176 <= nc.sbuf_usable_end
        yt = [at(f"yt{i}", [P, D], arena + 4096 * i) for i in range(NT + 1)]

        PS = ctx.enter_context(nc.psum_tensor("PS", [P, 8, 512], F32))

        def halves(t):
            return t[:, :].rearrange("p (a b) -> p a b", a=2)

        sems = {}

        def sem(name):
            if name not in sems:
                sems[name] = ctx.enter_context(nc.semaphore(name))
            return sems[name]

        once_in, once_dve, once_pe, once_act, once_out = (
            sem(n) for n in ("once_in", "once_dve", "once_pe", "once_act", "once_out"))
        const_set = sem("const_set")
        NONLAYER = len(sems)
        names = [
            "small_in", "low_in", "state_in", "bias_in0", "bias_in1", "cache_in0", "cache_in1", "bias_s_in",
            "x_hi", "x_lo", "squared", "sq_used", "ss_ready", "ms_ready", "low_scaled", "ss_all", "newton_act", "rstd_ready",
            "w_in0", "w_in1", "w_in2", "w_in3", "w_hi", "w_lo", "unit_done", "unit_read",
            "pe_low", "low_read", "pe_rms", "pe_z", "z_act", "z_min", "cum_ready",
            "r2_steps", "lev_x", "lev_f", "qk_pool", "qk_dve", "pe_lev", "lev_read",
            "pe_diag", "diag_read", "qe_act", "qe_dve", "kd_arg", "kd_act", "kd_ready", "dec_ready",
            "pe_tok", "tok_read", "pe_kv", "state_ready", "state_s_ready", "pe_out", "out_act", "out_dve",
            "pe_out_s", "outs_act", "outs_dve", "centred", "gn_var", "gn_act", "gn_done",
            "pe_back", "back_read", "rot_ready", "ret_scaled", "o_cleared", "s_cleared",
            "pe_heads", "heads_act", "heads_dve", "pe_score", "score_dve", "max_ready", "exp_done", "norm_done",
            "pe_score_s", "score_s_dve", "exp_s", "norm_s", "pe_turn", "turned", "pe_turn_s", "turned_s",
            "pe_pv", "pv_act", "pv_dve", "pe_pv_s", "pvs_act", "pvs_dve",
            "gate_act", "gate_dve", "cat_dve", "cat_hi", "cat_lo", "relu_ready", "z_hi", "z_lo", "out_dma", "stored0", "stored1", "dve_link", "act_link", "pool_link",
        ]
        for n in names:
            sem(n)
        layer_sems = [sems[n] for n in names]
        assert [s.num for s in layer_sems] == list(range(layer_sems[0].num, layer_sems[0].num + len(names)))

        xin = [at(f"xin{i}", [P, D], arena + 4096 * i) for i in range(5)]
        with nc.Block() as block:
            @block.sync
            def _(sp):
                for i in range(NT):
                    sp.dma_start(xin[i][:, :], x[i * P:(i + 1) * P, :]).then_inc(once_in, 16)
                sp.dma_start(xin[4][0:TS, :], x[TP:T, :]).then_inc(once_in, 16)
                for dst, src in ((cos_sb, cos_t), (sin_sb, sin_t), (reset_sb, reset), (lm_sb, lmask),
                                 (dm_sb, dmask), (qd_sb, qdec), (kd_sb, kdec), (sd_sb, sdec), (wf_sb, wf)):
                    sp.dma_start(dst[:], src).then_inc(once_in, 16)
                sp.wait_ge(once_in, 16 * 14)

            @block.gpsimd
            def _(pool):
                nc.gpsimd.memset(ident[:, :], 0.0).then_inc(const_set, 1)
                nc.gpsimd.memset(ones[:, :], 1.0).then_inc(const_set, 1)
                nc.gpsimd.memset(low_sb[:, :, :], 0.0).then_inc(const_set, 1)
                pool.wait_ge(const_set, 3)
                nc.gpsimd.affine_select(out=ident[:, :], in_=ident[:, :], compare_op=ALU.not_equal, fill=1.0,
                                        base=0, pattern=[[-1, P]], channel_multiplier=1).then_inc(const_set, 1)

            @block.tensor
            def _(pe):
                pe.wait_ge(const_set, 4)
                pe.wait_ge(once_in, 16 * 14)
                for kc in range(KC):
                    b = 2 * (kc % 4)
                    if kc >= 4:
                        pe.wait_ge(once_dve, 2 * (kc - 3))
                    for i in range(NT):
                        nc.tensor.transpose(PS[:, b, i * P:(i + 1) * P], xin[i][:, kc * P:(kc + 1) * P], ident[:, :])
                    nc.tensor.transpose(PS[:, b + 1, 0:TS], xin[4][0:TS, kc * P:(kc + 1) * P],
                                        ident[0:TS, 0:TS]).then_inc(once_pe, 1)

            @block.vector
            def _(dve):
                for kc in range(KC):
                    b = 2 * (kc % 4)
                    dve.wait_ge(once_pe, kc + 1)
                    nc.vector.tensor_copy(h[:, kc, 0:TP], PS[:, b, :]).then_inc(once_dve, 1)
                    nc.vector.tensor_copy(h[:, kc, TP:T], PS[:, b + 1, 0:TS]).then_inc(once_dve, 1)

        with nc.Fori(0, L) as layer:
            with nc.Block() as block:
                @block.sync
                def _(sp):
                    def load(n, j, first=False):
                        if not first:
                            sp.wait_ge(sems["w_lo"], n - RAW + 1)
                        sp.dma_start(raw[j][:, :], wu[layer * UNITS + n, :, :]).then_inc(sems[f"w_in{j}"], 16)

                    def state_in(kind):
                        if kind == RET:
                            sp.wait_ge(sems["state_s_ready"], 2)
                            sp.wait_ge(sems["outs_dve"], 2)
                            sp.wait_ge(sems["out_dma"], 16 * 4)
                        src = (st_gla, st_ret)[kind]
                        for g in range(2):
                            sp.dma_start(Ss[:, g, 0, :], src[layer, g, :, :]).then_inc(sems["state_in"], 16)

                    def band_in(u):
                        if u == 0:
                            sp.wait_ge(sems["rot_ready"], 4)
                            sp.wait_ge(sems["pe_tok"], 4)
                        for p in range(2):
                            if u >= 1:
                                sp.wait_ge(sems["score_dve"], 4 * (2 * (u - 1) + p + 1))
                            sp.dma_start(Bh[p][:, :], bias[layer, 2 * u + p, :, :]).then_inc(sems[f"bias_in{p}"], 16)
                        if u >= 2:
                            sp.wait_ge(sems["pe_heads"], u - 1)
                            sp.wait_ge(sems["pe_pv_s"], u - 1)
                        cols = slice(u * P, (u + 1) * P)
                        for dst, src in ((ckb, ck), (cvb, cv)):
                            sp.dma_start(dst[u % 2][:, :, :], src[layer, :, cols].rearrange("(j p) c -> p j c", p=P)) \
                                .then_inc(sems[f"cache_in{u % 2}"], 16)
                        if u >= 1:
                            sp.wait_ge(sems["score_s_dve"], 2 * u)
                        sp.dma_start(Bs[:, :], bias_s[layer, u, :, :]).then_inc(sems["bias_s_in"], 16)

                    sp.dma_start(sm[:, :], small[layer, :, :]).then_inc(sems["small_in"], 16)
                    load(0, 0, first=True)
                    sp.dma_start(low_sb[:, :, 0:16], w_low[layer, :, :, :]).then_inc(sems["low_in"], 16)
                    sp.dma_start(a2_sb[:, :], a2[layer, :, :]).then_inc(sems["low_in"], 16)
                    for n in range(1, RAW):
                        load(n, n, first=True)
                    state_in(GLA)
                    between = {12: lambda: state_in(RET), 15: lambda: band_in(0), 18: lambda: band_in(1),
                               21: lambda: band_in(2), 24: lambda: band_in(3)}
                    for n in range(RAW, N_IN + RAW):
                        if n - RAW in between:
                            between[n - RAW]()
                        load(n, n % RAW)
                    with sp.Fori(N_IN // RAW + 1, UNITS // RAW) as i:
                        for j in range(RAW):
                            load(i * RAW + j, j)
                    load(UNITS, 0)

                @block.gpsimd
                def _(pool):
                    links = [0]

                    def link(ins):
                        links[0] += 1
                        ins.then_inc(sems["pool_link"], 1)
                        pool.wait_ge(sems["pool_link"], links[0])

                    nc.gpsimd.memset(O[:, 16 * HD:], 0.0).then_inc(sems["o_cleared"], 1)
                    nc.gpsimd.memset(S[:, :, 0, :], 0.0).then_inc(sems["s_cleared"], 1)

                    def level(l):
                        H = LEVELS[l]
                        pool.wait_ge(sems["lev_f"], 2 * (l + 1))
                        if l >= 2:
                            pool.wait_ge(sems["pe_lev"], l - 1)
                        for g, c0, c1 in level_parts(H):
                            f, q, k = (blocks(t, c0, c1, H) for t in (F[l % 2], QK[l % 2], gk))
                            ins = nc.gpsimd.tensor_tensor(q[:, :, 0, :], f[:, :, 0, :], k[:, :, 0, :], ALU.mult)
                        ins.then_inc(sems["qk_pool"], 1)

                    pool.wait_ge(sems["unit_read"], 2)
                    for l in range(len(LEVELS)):
                        level(l)

                    for m in range(KC):
                        pool.wait_ge(sems["squared"], KC + m + 1)
                        if m:
                            pool.wait_ge(sems["sq_used"], m)
                            nc.gpsimd.tensor_tensor(ssum[:, :], ssum[:, :], sq[m % 2][:, :], ALU.add) \
                                .then_inc(sems["sq_used"], 1)
                        else:
                            nc.gpsimd.tensor_scalar(ssum[:, :], sq[0][:, :], 1.0, 0.0, ALU.mult, ALU.add) \
                                .then_inc(sems["sq_used"], 1)
                    pool.wait_ge(sems["sq_used"], KC)
                    nc.gpsimd.partition_all_reduce(rstd[:, :], ssum[:, :], P, RADD).then_inc(sems["ss_all"], 1)
                    with pool.Fori(0, GROUPS) as g:
                        for m in range(KC):
                            pool.wait_ge(sems["unit_read"], g * N_MLP + (N_IN + N_OUT + KC + m + 1))
                            nc.gpsimd.tensor_tensor(h[:, m, :], h[:, m, :], sq[m % 2][:, :], ALU.add) \
                                .then_inc(sems["sq_used"], 1)

                @block.scalar
                def _(act):
                    links = [0]

                    def link(ins):
                        links[0] += 1
                        ins.then_inc(sems["act_link"], 1)
                        act.wait_ge(sems["act_link"], links[0])

                    def split(n, g=0, first=False):
                        act.wait_ge(sems[f"w_in{n % RAW}"], g * (16 * N_MLP // RAW) + 16 * (n // RAW + 1))
                        if not first:
                            act.wait_ge(sems["unit_done"], g * N_MLP + (n - SPL + 1))
                        nc.scalar.activation(whi[n % SPL][:, :], raw[n % RAW][:, :], ACT.Copy).then_inc(sems["w_hi"], 1)

                    def xhi_tile(kc, w):
                        nc.scalar.activation(xhi[:, kc, :], h[:, kc, :], ACT.Copy, scale=sm[:, w + kc:w + kc + 1]) \
                            .then_inc(sems["x_hi"], 1)

                    def squares(kc):
                        if kc >= 2:
                            act.wait_ge(sems["ss_ready"], kc - 1)
                        nc.scalar.activation(sq[kc % 2][:, :], h[:, kc, :], ACT.Square).then_inc(sems["squared"], 1)

                    squares(0)
                    squares(1)
                    act.wait_ge(sems["small_in"], 16)
                    for kc in range(KC):
                        xhi_tile(kc, 0)
                        if kc < 2:
                            split(kc, first=True)
                        else:
                            squares(kc)
                    split(2)

                    def stage(st):
                        what = st[0]
                        if what == "rms":
                            act.wait_ge(sems["ms_ready"], 1)
                            link(nc.scalar.activation(nt[0][:, :], ssum[:, :], ACT.Ln))
                            nc.scalar.activation(nt[0][:, :], nt[0][:, :], ACT.Exp, scale=-0.5) \
                                .then_inc(sems["newton_act"], 1)
                        elif what == "z":
                            act.wait_ge(sems["z_min"], 2)
                            for g in range(2):
                                link(nc.scalar.activation(F[0][:, g * T:(g + 1) * T].rearrange("p (a b) -> p a b", a=2),
                                                          PS[:, M0 + 2 * g:M0 + 2 * g + 2, 0:HT], ACT.Abs,
                                                          bias=sm[:, 16 + g:17 + g]))
                            link(nc.scalar.activation(F[0][:, :], F[0][:, :], ACT.Exp, scale=-1.0))
                            nc.scalar.activation(F[0][:, :], F[0][:, :], ACT.Ln, bias=1.0).then_inc(sems["z_act"], 1)
                        elif what == "cum":
                            level_f(0)
                            level_f(1)
                            act.wait_ge(sems["cum_ready"], 2)
                            for g in range(2):
                                nc.scalar.activation(dec[:, g, 0:NC], gb[:, g * T + CH - 1:g * T + TP:CH], ACT.Exp,
                                                     scale=1.0 / 16)
                                ins = nc.scalar.activation(dec[:, g, NC:NC + 1], gb[:, (g + 1) * T - 1:(g + 1) * T],
                                                           ACT.Exp, scale=1.0 / 16)
                            ins.then_inc(sems["dec_ready"], 1)
                        elif what == "level":
                            if st[1] + 2 < len(LEVELS):
                                level_f(st[1] + 2)
                            else:
                                late_f(st[1] + 2 - len(LEVELS))
                        elif what == "tok":
                            _, kind, kv = st
                            n = 2 * kind + (kv == "k")
                            dst = (vtok, ktok)[kv == "k"]
                            act.wait_ge(sems["pe_tok"], n + 1)
                            for g in range(2):
                                nc.scalar.activation(dst[:, 0:NT, g * P:(g + 1) * P],
                                                     PS[:, M0 + g, :].rearrange("p (i c) -> p i c", c=P), ACT.Copy)
                            nc.scalar.activation(dst[0:TS, NT, :], PS[0:TS, M0 + 2, 0:256], ACT.Copy) \
                                .then_inc(sems["tok_read"], 1)
                        elif what == "out":
                            act.wait_ge(sems["pe_out"], st[1] + 1)
                            if st[1] == RET:
                                act.wait_ge(sems["back_read"], 2)
                            for p in range(2):
                                o_v = O[:, 0:16 * HD].rearrange("p (a b c) -> p a b c", b=2, c=HD)[:, :, p, :]
                                ins = nc.scalar.activation(o_v, PS[:, M0 + p, :].rearrange("p (a c) -> p a c", c=HD), ACT.Copy)
                            ins.then_inc(sems["out_act"], 1)
                        elif what == "out_s":
                            act.wait_ge(sems["o_cleared"], 1)
                            act.wait_ge(sems["pe_out_s"], st[1] + 1)
                            nc.scalar.activation(O[0:TS, 16 * HD:], PS[0:TS, M0, 0:256], ACT.Copy) \
                                .then_inc(sems["outs_act"], 1)
                            act.wait_ge(sems["outs_dve"], 2 * (st[1] + 1))
                            act.wait_ge(sems["out_dve"], 2 * (st[1] + 1))
                            if st[1] == RET:
                                act.wait_ge(sems["centred"], 1)
                            nc.scalar.activation(osq[:, :], O[:, :], ACT.Square).then_inc(sems["gn_act"], 1)
                        elif what == "gn":
                            act.wait_ge(sems["gn_var"], st[1] + 1)
                            link(nc.scalar.activation(gst[1][:, :], gst[0][:, :], ACT.Ln))
                            nc.scalar.activation(gst[1][:, :], gst[1][:, :], ACT.Exp, scale=-0.5) \
                                .then_inc(sems["gn_act"], 1)
                            act.wait_ge(sems["state_ready"], 16 * (st[1] + 1))
                            act.wait_ge(sems["state_s_ready"], 2 * (st[1] + 1))
                            dst, dst_s = ((gla_p, gla_s), (ret_p, ret_s))[st[1]]
                            for g in range(2):
                                act.dma_start(dst[layer, g, :, :], S[:, g, NC, :]).then_inc(sems["out_dma"], 16)
                                act.dma_start(dst_s[layer, g, :, :], Ss[:, g, 1, :]).then_inc(sems["out_dma"], 16)
                        elif what == "back":
                            kind = st[1]
                            act.wait_ge(sems["pe_back"], kind + 1)
                            for g in range(2):
                                j = 2 * (1 - kind) + g
                                nc.scalar.activation(oT[j][:, 0:TP], PS[:, M0 + g, :], ACT.Copy)
                                ins = nc.scalar.activation(oT[j][:, TP:T], PS[:, M0 + 2, g * TS:(g + 1) * TS], ACT.Copy)
                                ins.then_inc(sems["back_read"], 1)
                        elif what == "heads":
                            u = st[1]
                            act.wait_ge(sems["pe_heads"], u + 1)
                            if u >= 2:
                                act.wait_ge(sems["pe_pv_s"], u - 1)
                                act.wait_ge(sems[f"stored{u % 2}"], 64 * (u // 2))
                            if u >= 1:
                                act.wait_ge(sems["pe_score_s"], u)
                            s = u % 2
                            nc.scalar.activation(vtk[s][:, 0:NT, :], PS[:, M0, :].rearrange("p (i c) -> p i c", c=P), ACT.Copy)
                            nc.scalar.activation(vtk[s][0:TS, NT, :], PS[0:TS, M0 + 2, 0:P], ACT.Copy)
                            nc.scalar.activation(ktk[s][0:TS, NT, :], PS[0:TS, M0 + 2, P:2 * P], ACT.Copy)
                            nc.scalar.activation(ktk[s][:, 0:NT, :], PS[:, M0 + 1, :].rearrange("p (i c) -> p i c", c=P),
                                                 ACT.Copy).then_inc(sems["heads_act"], 1)
                            act.wait_ge(sems["heads_act"], u + 1)
                            cols = slice(u * P, (u + 1) * P)
                            for dst, dst_s, src in ((k_p, k_s, ktk[s]), (v_p, v_s, vtk[s])):
                                act.dma_start(dst[layer, :, cols].rearrange("(i p) c -> p i c", p=P), src[:, 0:NT, :]) \
                                    .then_inc(sems[f"stored{s}"], 16)
                                act.dma_start(dst_s[layer, :, cols], src[0:TS, NT, :]).then_inc(sems[f"stored{s}"], 16)
                        elif what == "score":
                            _, u, p = st
                            act.wait_ge(sems["max_ready"], 2 * u + p + 1)
                            for i in range(NT):
                                r = Pr[p][:, P_OFF[i]:P_OFF[i] + (i + 1) * P]
                                ins = nc.scalar.activation(r, r, ACT.Exp, bias=mx[:, p, i:i + 1], accum_out=rs[:, p, i:i + 1])
                            ins.then_inc(sems["exp_done"], 1)
                        elif what == "score_s":
                            act.wait_ge(sems["score_s_dve"], 2 * (st[1] + 1))
                            nc.scalar.activation(Prs[:, :], Prs[:, :], ACT.Exp, bias=mxs[:, 0:1], accum_out=rss[:, 0:1]) \
                                .then_inc(sems["exp_s"], 1)
                        elif what == "turn":
                            _, u, p = st
                            n = 2 * u + p
                            if n == 0:
                                act.wait_ge(sems["out_dma"], 16 * 8)
                            act.wait_ge(sems["pe_turn"], n + 1)
                            if u >= 1:
                                act.wait_ge(sems["pe_pv"], u)
                            for b in range(3):
                                c0, c1 = TURN_COLS[b]
                                nc.scalar.activation(PT[p][:, c0:c1], PS[:, M0 + b, 0:c1 - c0], ACT.Copy) \
                                    .then_inc(sems["turned"], 1)
                        elif what == "turn_s":
                            u = st[1]
                            act.wait_ge(sems["pe_turn_s"], u + 1)
                            nc.scalar.activation(PTs[:, 0:NT, :], PS[:, M0 + 3, 0:256].rearrange("p (j c) -> p j c", c=64), ACT.Copy)
                            nc.scalar.activation(PTs[0:TS, NT, :], PS[0:TS, M0 + 3, 256:320], ACT.Copy) \
                                .then_inc(sems["turned_s"], 1)
                        elif what == "pv":
                            u = st[1]
                            act.wait_ge(sems["pe_pv"], u + 1)
                            nc.scalar.activation(zhi[:, 4 + u, 0:TP], PS[:, M0 + 0, :], ACT.Copy).then_inc(sems["pv_act"], 1)
                        elif what == "pv_s":
                            u = st[1]
                            act.wait_ge(sems["pe_pv_s"], u + 1)
                            nc.scalar.activation(zhi[:, 4 + u, TP:T], PS[:, M0 + 3, 0:TS], ACT.Copy).then_inc(sems["pvs_act"], 1)

                    def level_f(l):
                        H = LEVELS[l]
                        act.wait_ge(sems["lev_x"], l + 1)
                        parts = level_parts(H)
                        for side, sc in ((0, -1.0 / 16), (1, 1.0 / 16)):
                            for g, c0, c1 in parts:
                                f = blocks(F[l % 2], c0, c1, H)
                                ins = nc.scalar.activation(f[:, :, side, :], f[:, :, side, :], ACT.Exp, scale=sc)
                            ins.then_inc(sems["lev_f"], 1)

                    def late_f(which):
                        if which == 0:
                            nc.scalar.activation(qe_g[:, :], gb[:, :], ACT.Exp, scale=1.0 / 16).then_inc(sems["qe_act"], 1)
                        else:
                            act.wait_ge(sems["kd_arg"], 1)
                            nc.scalar.activation(F[0][:, :], F[0][:, :], ACT.Exp, scale=1.0 / 16).then_inc(sems["kd_act"], 1)

                    def new_x(m):
                        act.wait_ge(sems["unit_read"], N_IN + m + 1)
                        xhi_tile(m, KC)
                        if m >= 2:
                            act.wait_ge(sems["sq_used"], m - 1)
                        nc.scalar.activation(sq[m % 2][:, :], h[:, m, :], ACT.Square).then_inc(sems["squared"], 1)

                    def relu(k, g):
                        n = N_IN + N_OUT + k
                        r = nt[k % 2]
                        act.wait_ge(sems["unit_done"], g * N_MLP + (n + 1))
                        if k >= 2:
                            act.wait_ge(sems["z_lo"], g * KC + (k - 1))
                        nc.scalar.activation(halves(r), PS[:, 2 * (n % 2):2 * (n % 2) + 2, 0:HT], ACT.Relu) \
                            .then_inc(sems["relu_ready"], 1)
                        act.wait_ge(sems["unit_read"], g * N_MLP + (n + 1))
                        nc.scalar.activation(zhi[:, k, :], r[:, :], ACT.Copy).then_inc(sems["z_hi"], 1)

                    def gate(j):
                        e = sq[j % 2]
                        act.wait_ge(sems["unit_read"], GATE + j + 1)
                        if j >= 2:
                            act.wait_ge(sems["gate_dve"], 2 * (j - 1))
                        link(nc.scalar.activation(e[:, :], G[j][:, :], ACT.Abs))
                        link(nc.scalar.activation(e[:, :], e[:, :], ACT.Exp, scale=-1.0))
                        nc.scalar.activation(e[:, :], e[:, :], ACT.Ln, bias=1.0).then_inc(sems["gate_act"], 1)
                        act.wait_ge(sems["gate_dve"], 2 * j + 1)
                        nc.scalar.activation(e[:, :], e[:, :], ACT.Exp).then_inc(sems["gate_act"], 1)
                        act.wait_ge(sems["cat_dve"], j + 1)
                        nc.scalar.activation(zhi[:, j, :], G[j][:, :], ACT.Copy).then_inc(sems["cat_hi"], 1)

                    for n, half in SLOTS:
                        if half == 0:
                            split(n + 1)
                        for st in ACT_STEPS.get((n, half), []):
                            stage(st)
                        if half == 1 and n > GATE:
                            gate(n - GATE - 1)
                    for m in range(KC):
                        split(N_IN + m + 1)
                        if m == 0:
                            stage(("pv_s", 3))
                            gate(3)
                        else:
                            new_x(m - 1)
                    new_x(KC - 1)
                    with act.Fori(0, GROUPS) as g:
                        for k in range(N_MLP):
                            n = N_IN + N_OUT + k
                            split(n + 1, g)
                            if 1 <= k <= KC:
                                relu(k - 1, g)
                    act.wait_ge(sems["out_dma"], 16 * 8)
                    for s in range(2):
                        act.wait_ge(sems[f"stored{s}"], 64 * 2)

                @block.vector
                def _(dve):
                    links = [0]

                    def link(ins):
                        links[0] += 1
                        ins.then_inc(sems["dve_link"], 1)
                        dve.wait_ge(sems["dve_link"], links[0])

                    def rest(n, g=0):
                        dve.wait_ge(sems["w_hi"], g * N_MLP + (n + 1))
                        nc.vector.tensor_tensor(wlo[n % SPL][:, :], raw[n % RAW][:, :], f32(whi[n % SPL][:, :]),
                                                ALU.subtract).then_inc(sems["w_lo"], 1)

                    def xlo_tile(kc, w, count):
                        dve.wait_ge(sems["x_hi"], count)
                        nc.vector.scalar_tensor_tensor(xlo[:, kc, :], h[:, kc, :], sm[:, w + kc:w + kc + 1],
                                                       f32(xhi[:, kc, :]), ALU.mult, ALU.subtract) \
                            .then_inc(sems["x_lo"], 1)

                    def newton(y, v, out, t):
                        link(nc.vector.tensor_tensor(t, y, y, ALU.mult))
                        link(nc.vector.tensor_tensor(t, t, v, ALU.mult))
                        link(nc.vector.tensor_scalar(t, t, -0.5, 1.5, ALU.mult, ALU.add))
                        return nc.vector.tensor_tensor(out, y, t, ALU.mult)

                    def add_square(kc):
                        dve.wait_ge(sems["squared"], kc + 1)
                        if kc == 0:
                            nc.vector.tensor_copy(ssum[:, :], sq[0][:, :]).then_inc(sems["ss_ready"], 1)
                        else:
                            dve.wait_ge(sems["ss_ready"], kc)
                            nc.vector.tensor_tensor(ssum[:, :], ssum[:, :], sq[kc % 2][:, :], ALU.add) \
                                .then_inc(sems["ss_ready"], 1)

                    add_square(0)
                    add_square(1)
                    dve.wait_ge(sems["small_in"], 16)
                    for kc in range(KC):
                        xlo_tile(kc, 0, kc + 1)
                        if kc < 2:
                            rest(kc)
                        else:
                            add_square(kc)
                    dve.wait_ge(sems["low_in"], 32)
                    nc.vector.tensor_tensor(low_sb[:, :, :], low_sb[:, :, :],
                                            sm[:, 0:KC].unsqueeze(2).to_broadcast([P, KC, 32]), ALU.mult) \
                        .then_inc(sems["low_scaled"], 1)

                    def unit_out(n):
                        src = PS[:, bank(n):bank(n) + 2, 0:HT]
                        dve.wait_ge(sems["unit_done"], n + 1)
                        if n == 0:
                            dve.wait_ge(sems["rstd_ready"], 1)

                        if n == RQ:
                            dve.wait_ge(sems["rot_ready"], 2)

                        def out(dst, by):
                            return nc.vector.tensor_tensor(dst, src, by, ALU.mult)

                        if n in (GQ, GQ + 1):
                            d = gq[:, (n - GQ) * T:(n - GQ + 1) * T].rearrange("p (a b) -> p a b", a=2)
                            ins = nc.vector.scalar_tensor_tensor(d, src, HD ** -0.5, halves(rstd), ALU.mult, ALU.mult)
                        elif n in (RK, RQ):
                            if n == RK:
                                link(nc.vector.tensor_tensor(nt[0][:, :], cos_sb[:, :], rstd[:, :], ALU.mult))
                                link(nc.vector.tensor_tensor(nt[1][:, :], sin_sb[:, :], rstd[:, :], ALU.mult))
                            link(out(halves(rot[0]), halves(nt[0])))
                            ins = out(halves(rot[1]), halves(nt[1]))
                        elif n in (RK + 1, RQ + 1):
                            link(out(halves(sq[0]), halves(nt[1])))
                            ins = out(halves(sq[1]), halves(nt[0]))
                        elif n >= GATE:
                            ins = out(halves(G[n - GATE]), halves(rstd))
                        elif n >= AQ:
                            u, which = divmod(n - AQ, 3)
                            d = halves(qkv[u % 2][which])
                            if which == 0:
                                ins = nc.vector.scalar_tensor_tensor(d, src, HD ** -0.5, halves(rstd), ALU.mult, ALU.mult)
                            else:
                                ins = out(d, halves(rstd))
                        else:
                            d, first = {0: (gk, GK), 1: (gk, GK), 4: (gv, GV), 5: (gv, GV), 10: (rv, RV), 11: (rv, RV)}[n]
                            ins = out(d[:, (n - first) * T:(n - first + 1) * T].rearrange("p (a b) -> p a b", a=2),
                                      halves(rstd))
                        ins.then_inc(sems["unit_read"], 1)

                    def rotary(first, g):
                        dst = rk if first == RK else rq
                        dve.wait_ge(sems["unit_read"], first + 2)
                        c = slice(g * T, (g + 1) * T)
                        for p in range(2):
                            s32 = slice(32 * (2 * g + p), 32 * (2 * g + p) + 32)
                            nc.vector.tensor_tensor(dst[64 * p:64 * p + 32, c], rot[0][s32, :], sq[0][s32, :], ALU.subtract)
                            ins = nc.vector.tensor_tensor(dst[64 * p + 32:64 * p + 64, c], rot[1][s32, :],
                                                          sq[1][s32, :], ALU.add)
                        ins.then_inc(sems["rot_ready"], 1)

                    def level_x(l):
                        H = LEVELS[l]
                        if l >= 2:
                            dve.wait_ge(sems["qk_pool"], l - 1)
                        for g, c0, c1 in level_parts(H):
                            f, b = blocks(F[l % 2], c0, c1, H), blocks(gb, c0, c1, H)
                            nb = (c1 - c0) // (2 * H)
                            ref = b[:, :, 0:1, H - 1:H].rearrange("p b x h -> p b (x h)").to_broadcast([P, nb, 2 * H])
                            ins = nc.vector.tensor_tensor(f.rearrange("p b x h -> p b (x h)"),
                                                          b.rearrange("p b x h -> p b (x h)"), ref, ALU.subtract)
                        ins.then_inc(sems["lev_x"], 1)

                    def level_q(l):
                        H = LEVELS[l]
                        dve.wait_ge(sems["lev_f"], 2 * (l + 1))
                        if l >= 2:
                            dve.wait_ge(sems["pe_lev"], l - 1)
                        for g, c0, c1 in level_parts(H):
                            f, q, k = (blocks(t, c0, c1, H) for t in (F[l % 2], QK[l % 2], gq))
                            ins = nc.vector.tensor_tensor(q[:, :, 1, :], f[:, :, 1, :], k[:, :, 1, :], ALU.mult)
                        ins.then_inc(sems["qk_dve"], 1)

                    def stage(st):
                        what = st[0]
                        if what == "rotary":
                            rotary(st[1], st[2])
                        elif what == "rms":
                            dve.wait_ge(sems["pe_rms"], 1)
                            nc.vector.tensor_scalar(halves(ssum), PS[:, M0 + 2:M0 + 4, 0:HT], 1.0 / D, EPS,
                                                    ALU.mult, ALU.add).then_inc(sems["ms_ready"], 1)
                            rest(2)
                            dve.wait_ge(sems["ms_ready"], 1)
                            dve.wait_ge(sems["newton_act"], 1)
                            newton(nt[0][:, :], ssum[:, :], rstd[:, :], nt[1][:, :]).then_inc(sems["rstd_ready"], 1)
                            dve.wait_ge(sems["rstd_ready"], 1)
                            unit_out(0)
                            unit_out(1)
                            dve.wait_ge(sems["pe_low"], 1)
                            nc.vector.tensor_tensor(F[1][:, 0:T].rearrange("p (a b) -> p a b", a=2),
                                                    PS[:, M0:M0 + 2, 0:HT], halves(rstd), ALU.mult) \
                                .then_inc(sems["low_read"], 1)
                        elif what == "z":
                            dve.wait_ge(sems["pe_z"], 1)
                            for g in range(2):
                                nc.vector.tensor_scalar(gb[:, g * T:(g + 1) * T].rearrange("p (a b) -> p a b", a=2),
                                                        PS[:, M0 + 2 * g:M0 + 2 * g + 2, 0:HT], sm[:, 16 + g:17 + g], 0.0,
                                                        ALU.add, ALU.min).then_inc(sems["z_min"], 1)
                        elif what == "cum":
                            dve.wait_ge(sems["z_min"], 2)
                            dve.wait_ge(sems["z_act"], 1)
                            link(nc.vector.tensor_tensor(gb[:, :], gb[:, :], F[0][:, :], ALU.subtract))
                            for g in range(2):
                                c = slice(g * T, (g + 1) * T)
                                nc.vector.tensor_tensor_scan(gb[:, c], reset_sb[:, :], gb[:, c], 0.0, ALU.mult, ALU.add) \
                                    .then_inc(sems["cum_ready"], 1)
                            dve.wait_ge(sems["cum_ready"], 2)
                            level_x(0)
                            level_x(1)
                        elif what == "diag":
                            kind = st[1]
                            if kind == GLA:
                                level_q(0)
                            dve.wait_ge(sems["pe_diag"], kind + 1)
                            for p in range(2):
                                nc.vector.tensor_tensor(
                                    Pm[:, 8 * p:8 * p + 8, :].rearrange("p (g i) c -> p g i c", g=2),
                                    PS[:, M0 + p, :].rearrange("p (g i c) -> p g i c", g=2, c=CH),
                                    dm_sb[:, kind, 2 * p:2 * p + 2, :].unsqueeze(2).to_broadcast([P, 2, NT, CH]), ALU.mult)
                                ins = nc.vector.tensor_tensor(
                                    Ps[:, 2 * p:2 * p + 2, :], PS[0:TS, M0 + 2 + p, 0:2 * TS].rearrange("p (g c) -> p g c", g=2),
                                    dm_sb[0:TS, kind, 2 * p:2 * p + 2, 0:TS], ALU.mult)
                            ins.then_inc(sems["diag_read"], 1)
                            dve.wait_ge(sems["diag_read"], kind + 1)
                            if kind == RET:
                                for t, tab, s0 in ((rq, qd_sb, 0), (rk, kd_sb, CH)):
                                    for g in range(2):
                                        c = t[:, g * T:g * T + TP].rearrange("p (n c) -> p n c", c=CH)
                                        nc.vector.tensor_tensor(c, c, tab[:, g:g + 1, 0:CH].to_broadcast([P, NC, CH]), ALU.mult)
                                        c = t[:, g * T + TP:(g + 1) * T]
                                        ins = nc.vector.tensor_tensor(c, c, tab[:, g, s0:s0 + TS], ALU.mult)
                                    ins.then_inc(sems["ret_scaled"], 1)
                        elif what == "level":
                            l = st[1]
                            H = LEVELS[l]
                            if l + 1 < len(LEVELS):
                                level_q(l + 1)
                            if l + 2 < len(LEVELS):
                                level_x(l + 2)
                            elif l + 2 == len(LEVELS):
                                dve.wait_ge(sems["qk_pool"], 5)
                                for g in range(2):
                                    b, f = (t[:, g * T:g * T + TP].rearrange("p (n c) -> p n c", c=CH) for t in (gb, F[0]))
                                    nc.vector.tensor_tensor(f, b[:, :, CH - 1:CH].to_broadcast([P, NC, CH]), b, ALU.subtract)
                                    b, f = (t[:, g * T + TP:(g + 1) * T] for t in (gb, F[0]))
                                    ins = nc.vector.tensor_tensor(f, b[:, TS - 1:TS].to_broadcast([P, TS]), b, ALU.subtract)
                                ins.then_inc(sems["kd_arg"], 1)
                            dve.wait_ge(sems["pe_lev"], l + 1)
                            b0 = 2 * (l % 2)
                            for p in range(2):
                                nb = CH // (2 * H)
                                out = Pm[:, 8 * p:8 * p + 8, :].rearrange("p s (b x h) -> p s b x h", x=2, h=H)[:, :, :, 1, :]
                                m = lm_sb[:, l:l + 1, :].to_broadcast([P, 8, 32]).rearrange("p s (b h) -> p s b h", h=H)
                                ins = nc.vector.copy_predicated(out, m, PS[:, M0 + b0 + p, 0:256]
                                                                .rearrange("p (s b h) -> p s b h", s=8, h=H))
                                if H <= TS // 2:
                                    out = Ps[:, 2 * p:2 * p + 2, :].rearrange("p s (b x h) -> p s b x h", x=2, h=H)[:, :, :, 1, :]
                                    m = lm_sb[0:TS, l:l + 1, 0:16].to_broadcast([TS, 2, 16]).rearrange("p s (b h) -> p s b h", h=H)
                                    ins = nc.vector.copy_predicated(out, m, PS[0:TS, M0 + b0 + p, 256:288]
                                                                    .rearrange("p (s b h) -> p s b h", s=2, h=H))
                            ins.then_inc(sems["lev_read"], 1)
                            dve.wait_ge(sems["lev_read"], l + 1)
                            if l + 1 == len(LEVELS):
                                dve.wait_ge(sems["qe_act"], 1)
                                nc.vector.tensor_tensor(qe_g[:, :], qe_g[:, :], gq[:, :], ALU.mult).then_inc(sems["qe_dve"], 1)
                                dve.wait_ge(sems["kd_act"], 1)
                                nc.vector.tensor_tensor(F[0][:, :], F[0][:, :], gk[:, :], ALU.mult).then_inc(sems["kd_ready"], 1)
                        elif what == "kv":
                            kind = st[1]
                            dve.wait_ge(sems["pe_kv"], kind + 1)
                            dve.wait_ge(sems["s_cleared"], 1)
                            dve.wait_ge(sems["dec_ready"], 1)
                            if kind == RET:
                                dve.wait_ge(sems["pe_out"], 1)
                                dve.wait_ge(sems["out_dma"], 16 * 4)
                            for c in range(NC):
                                for g in range(2):
                                    by = dec[:, g, c:c + 1] if kind == GLA else sd_sb[:, g, 0:1]
                                    o = (2 * (c // 2) + g) * HD
                                    nc.vector.scalar_tensor_tensor(S[:, g, c + 1, :], S[:, g, c, :], by,
                                                                   PS[:, M0 + c % 2, o:o + HD], ALU.mult, ALU.add) \
                                        .then_inc(sems["state_ready"], 1)
                                if c + 1 < NC:
                                    dve.wait_ge(sems["state_ready"], 2 * NC * kind + 2 * (c + 1))
                            dve.wait_ge(sems["state_in"], 32 * (kind + 1))
                            for g in range(2):
                                by = dec[:, g, NC:NC + 1] if kind == GLA else sd_sb[:, g, 1:2]
                                nc.vector.scalar_tensor_tensor(Ss[:, g, 1, :], Ss[:, g, 0, :], by,
                                                               PS[:, M0 + 2, g * HD:(g + 1) * HD], ALU.mult, ALU.add) \
                                    .then_inc(sems["state_s_ready"], 1)
                        elif what == "out":
                            dve.wait_ge(sems["out_act"], st[1] + 1)
                            for p in range(2):
                                o_v = O[:, 0:16 * HD].rearrange("p (a b c) -> p a b c", b=2, c=HD)[:, :, p, :]
                                nc.vector.tensor_tensor(o_v, PS[:, M0 + 2 + p, :].rearrange("p (a c) -> p a c", c=HD), o_v,
                                                        ALU.add).then_inc(sems["out_dve"], 1)
                        elif what == "out_s":
                            kind = st[1]
                            dve.wait_ge(sems["outs_act"], kind + 1)
                            for p in range(2):
                                o_v = O[0:TS, 16 * HD:].rearrange("p (a b c) -> p a b c", b=2, c=HD)[:, :, p, :]
                                nc.vector.tensor_tensor(o_v, PS[0:TS, M0 + 1 + p, 0:2 * HD].rearrange("p (a c) -> p a c", c=HD),
                                                        o_v, ALU.add).then_inc(sems["outs_dve"], 1)
                            o_v = O[:, :].rearrange("p (a c) -> p a c", c=HD)
                            dve.wait_ge(sems["outs_dve"], 2 * (kind + 1))
                            dve.wait_ge(sems["out_dve"], 2 * (kind + 1))
                            if kind == RET:
                                link(nc.vector.reduce_sum(gst[2][:, :], o_v, AX_X))
                                link(nc.vector.tensor_scalar(gst[2][:, :], gst[2][:, :], 1.0 / HD, None, ALU.mult))
                                nc.vector.tensor_tensor(o_v, o_v, gst[2][:, :].unsqueeze(2).to_broadcast([P, 20, HD]),
                                                        ALU.subtract).then_inc(sems["centred"], 1)
                        elif what == "gn":
                            kind = st[1]
                            o_v = O[:, :].rearrange("p (a c) -> p a c", c=HD)
                            dve.wait_ge(sems["gn_act"], 2 * kind + 1)
                            link(nc.vector.reduce_sum(gst[0][:, :], osq[:, :].rearrange("p (a c) -> p a c", c=HD), AX_X))
                            nc.vector.tensor_scalar(gst[0][:, :], gst[0][:, :], 1.0 / HD, EPS, ALU.mult, ALU.add) \
                                .then_inc(sems["gn_var"], 1)
                            dve.wait_ge(sems["gn_var"], kind + 1)
                            dve.wait_ge(sems["gn_act"], 2 * kind + 2)
                            link(newton(gst[1][:, :], gst[0][:, :], gst[1][:, :], gst[2][:, :]))
                            nc.vector.tensor_tensor(o_v, o_v, gst[1][:, :].unsqueeze(2).to_broadcast([P, 20, HD]), ALU.mult) \
                                .then_inc(sems["gn_done"], 1)
                        elif what == "heads":
                            u = st[1]
                            dve.wait_ge(sems["pe_heads"], u + 1)
                            if u >= 1:
                                dve.wait_ge(sems["pe_score_s"], u)
                            nc.vector.tensor_copy(kct[:, :], PS[:, M0 + 3, :]).then_inc(sems["heads_dve"], 1)
                        elif what == "score":
                            _, u, p = st
                            k = 2 * u + p
                            dve.wait_ge(sems[f"bias_in{p}"], 16 * (u + 1))
                            if u >= 1:
                                dve.wait_ge(sems["pe_turn"], 2 * (u - 1) + p + 1)
                            dve.wait_ge(sems["pe_score"], k + 1)
                            for i, b, c in SCORE:
                                w = (i + 1) * P
                                nc.vector.tensor_tensor_reduce(
                                    out=Pr[p][:, P_OFF[i]:P_OFF[i] + w], in0=PS[:, M0 + b, c:c + w], in1=Bh[p][:, TP - w:TP],
                                    scale=1.0, scalar=-3e38, op0=ALU.add, op1=ALU.max, accum_out=mx[:, p, i:i + 1]) \
                                    .then_inc(sems["score_dve"], 1)
                            dve.wait_ge(sems["score_dve"], 4 * (k + 1))
                            nc.vector.tensor_scalar(mx[:, p, :], mx[:, p, :], -1.0, None, ALU.mult).then_inc(sems["max_ready"], 1)
                        elif what == "norm":
                            _, u, p = st
                            dve.wait_ge(sems["exp_done"], 2 * u + p + 1)
                            link(nc.vector.reciprocal(rs[:, p, :], rs[:, p, :]))
                            for i in range(NT):
                                r = Pr[p][:, P_OFF[i]:P_OFF[i] + (i + 1) * P]
                                ins = nc.vector.tensor_scalar(r, r, rs[:, p, i:i + 1], None, ALU.mult)
                            ins.then_inc(sems["norm_done"], 1)
                        elif what == "score_s":
                            u = st[1]
                            dve.wait_ge(sems["bias_s_in"], 16 * (u + 1))
                            if u >= 1:
                                dve.wait_ge(sems["pe_turn_s"], u)
                            dve.wait_ge(sems["pe_score_s"], u + 1)
                            link(nc.vector.tensor_tensor(Prs[:, 0:TP], PS[0:64, M0 + 3, :], Bs[:, 0:TP], ALU.add))
                            nc.vector.tensor_tensor(Prs[:, TP:T], PS[64:P, M0 + 3, 0:TS], Bs[:, TP:T], ALU.add) \
                                .then_inc(sems["score_s_dve"], 1)
                            dve.wait_ge(sems["score_s_dve"], 2 * u + 1)
                            nc.vector.tensor_reduce(mxs[:, :], Prs[:, :], AX_X, ALU.max, negate=True) \
                                .then_inc(sems["score_s_dve"], 1)
                        elif what == "norm_s":
                            dve.wait_ge(sems["exp_s"], st[1] + 1)
                            link(nc.vector.reciprocal(rss[:, :], rss[:, :]))
                            nc.vector.tensor_scalar(Prs[:, :], Prs[:, :], rss[:, 0:1], None, ALU.mult).then_inc(sems["norm_s"], 1)
                        elif what == "pv":
                            u = st[1]
                            dve.wait_ge(sems["pv_act"], u + 1)
                            nc.vector.tensor_tensor(zlo[:, 4 + u, 0:TP], PS[:, M0, :], f32(zhi[:, 4 + u, 0:TP]), ALU.subtract) \
                                .then_inc(sems["pv_dve"], 1)
                        elif what == "pv_s":
                            u = st[1]
                            dve.wait_ge(sems["pvs_act"], u + 1)
                            nc.vector.tensor_tensor(zlo[:, 4 + u, TP:T], PS[:, M0 + 3, 0:TS], f32(zhi[:, 4 + u, TP:T]),
                                                    ALU.subtract).then_inc(sems["pvs_dve"], 1)

                    def gate(j):
                        e = sq[j % 2]
                        dve.wait_ge(sems["gate_act"], 2 * j + 1)
                        dve.wait_ge(sems["unit_read"], GATE + j + 1)
                        nc.vector.scalar_tensor_tensor(e[:, :], G[j][:, :], 0.0, e[:, :], ALU.min, ALU.subtract) \
                            .then_inc(sems["gate_dve"], 1)
                        dve.wait_ge(sems["gate_act"], 2 * j + 2)
                        nc.vector.scalar_tensor_tensor(G[j][:, :], G[j][:, :], sm[:, 18 + j:19 + j], e[:, :],
                                                       ALU.mult, ALU.mult).then_inc(sems["gate_dve"], 1)
                        dve.wait_ge(sems["gate_dve"], 2 * j + 2)
                        dve.wait_ge(sems["back_read"], 4)
                        nc.vector.tensor_tensor(G[j][:, :], G[j][:, :], oT[j][:, :], ALU.mult).then_inc(sems["cat_dve"], 1)
                        dve.wait_ge(sems["cat_hi"], j + 1)
                        nc.vector.tensor_tensor(zlo[:, j, :], G[j][:, :], f32(zhi[:, j, :]), ALU.subtract) \
                            .then_inc(sems["cat_lo"], 1)

                    for n, half in SLOTS:
                        if half == 0 and n >= 3:
                            unit_out(n - 1)
                        for st in DVE_STEPS.get((n, half), []):
                            stage(st)
                        if half == 0:
                            rest(n + 1)
                        if half == 1 and n > GATE:
                            gate(n - GATE - 1)

                    def residual(m):
                        n = N_IN + m
                        dve.wait_ge(sems["unit_done"], n + 1)
                        hv = h[:, m, :].rearrange("p (a b) -> p a b", a=2)
                        nc.vector.tensor_tensor(hv, PS[:, 2 * (n % 2):2 * (n % 2) + 2, 0:HT], hv, ALU.add) \
                            .then_inc(sems["unit_read"], 1)
                        xlo_tile(m, KC, KC + m + 1)

                    for m in range(KC):
                        rest(N_IN + m + 1)
                        if m == 0:
                            unit_out(N_IN - 1)
                            stage(("pv_s", 3))
                            gate(3)
                        else:
                            residual(m - 1)
                    residual(KC - 1)

                    def square(k, g):
                        n = N_IN + N_OUT + k
                        r = nt[k % 2]
                        dve.wait_ge(sems["relu_ready"], g * KC + (k + 1))
                        nc.vector.scalar_tensor_tensor(halves(r), PS[:, 2 * (n % 2):2 * (n % 2) + 2, 0:HT], 0.0, halves(r),
                                                       ALU.max, ALU.mult).then_inc(sems["unit_read"], 1)
                        dve.wait_ge(sems["z_hi"], g * KC + (k + 1))
                        nc.vector.tensor_tensor(zlo[:, k, :], r[:, :], f32(zhi[:, k, :]), ALU.subtract) \
                            .then_inc(sems["z_lo"], 1)

                    def scaled(m, g):
                        n = N_IN + N_OUT + KC + m
                        dve.wait_ge(sems["unit_done"], g * N_MLP + (n + 1))
                        dve.wait_ge(sems["sq_used"], g * KC + (KC + m - 1))
                        nc.vector.tensor_tensor(halves(sq[m % 2]), PS[:, 2 * (n % 2):2 * (n % 2) + 2, 0:HT], halves(r2),
                                                ALU.mult).then_inc(sems["unit_read"], 1)

                    with dve.Fori(0, GROUPS) as g:
                        for k in range(N_MLP):
                            rest(N_IN + N_OUT + k + 1, g)
                            if 1 <= k <= KC:
                                square(k - 1, g)
                            elif k > KC:
                                scaled(k - 1 - KC, g)
                            if k == 4:
                                dve.wait_ge(sems["ss_all"], 1)
                                nc.vector.tensor_scalar(r2[:, :], rstd[:, :], 1.0 / D, EPS, ALU.mult, ALU.add) \
                                    .then_inc(sems["r2_steps"], 1)
                            if k in (5, 6):
                                c = slice((k - 5) * HT, (k - 4) * HT)
                                dve.wait_ge(sems["r2_steps"], g * 3 + (k - 4))
                                nc.vector.reciprocal(r2[:, c], r2[:, c]).then_inc(sems["r2_steps"], 1)
                        dve.wait_ge(sems["r2_steps"], g * 3 + 3)
                        scaled(KC - 1, g)

                @block.tensor
                def _(pe):
                    freed = {}

                    def take(*banks):
                        for b in banks:
                            if b in freed:
                                pe.wait_ge(sems[freed[b][0]], freed[b][1])

                    def give(banks, name, count):
                        for b in banks:
                            freed[b] = (name, count)

                    def mm(out, lhsT, rhs, start=True, stop=True):
                        return nc.tensor.matmul(out, lhsT, rhs, start=start, stop=stop, skip_group_check=True)

                    def begin(n, g=0):
                        pe.wait_ge(sems["w_lo"], g * N_MLP + (n + 1))
                        if n == 2:
                            pe.wait_ge(sems["ms_ready"], 1)
                        elif n > 2:
                            pe.wait_ge(sems["unit_read"], g * N_MLP + (n - 1))

                    def products(n, src, kcs, first=True, last=True, parts=(0, 1), ready=None):
                        (hi, lo), b, s = src, bank(n), n % SPL
                        for a in parts:
                            c, o = slice(a * HT, (a + 1) * HT), PS[:, b + a, 0:HT]
                            for kc in kcs:
                                if ready is not None and a == 0:
                                    ready(kc)
                                w = slice(kc * P, (kc + 1) * P)
                                mm(o, whi[s][:, w], hi[:, kc, c], first and kc == kcs[0], False)
                                mm(o, whi[s][:, w], lo[:, kc, c], False, False)
                                ins = mm(o, wlo[s][:, w], hi[:, kc, c], False, last and kc == kcs[-1])
                        if last and parts[-1] == 1:
                            ins.then_inc(sems["unit_done"], 1)

                    def chunks():
                        for p in range(2):
                            for g in range(2):
                                for c in range(NC):
                                    yield p, g, c

                    def stage(st):
                        what = st[0]
                        if what == "low":
                            pe.wait_ge(sems["low_scaled"], 1)
                            for kk in range(2):
                                for a in range(2):
                                    for j in range(4):
                                        last = mm(PS[32 * j:32 * j + 32, M0 + a, 0:HT], low_sb[:, 2 * j + kk, :],
                                                  h[:, 2 * j + kk, a * HT:(a + 1) * HT], kk == 0, kk == 1)
                            last.then_inc(sems["pe_low"], 1)
                            give((0, 1), "low_read", 1)
                        elif what == "rms":
                            pe.wait_ge(sems["ss_ready"], KC)
                            for a in range(2):
                                last = mm(PS[:, M0 + 2 + a, 0:HT], ones[:, :], ssum[:, a * HT:(a + 1) * HT])
                            last.then_inc(sems["pe_rms"], 1)
                            give((2, 3), "ms_ready", 1)
                        elif what == "z":
                            take(0, 1)
                            pe.wait_ge(sems["unit_read"], 3)
                            for g in range(2):
                                for a in range(2):
                                    last = mm(PS[:, M0 + 2 * g + a, 0:HT], a2_sb[:, g * P:(g + 1) * P],
                                              F[1][:, a * HT:(a + 1) * HT])
                            last.then_inc(sems["pe_z"], 1)
                            give((0, 1, 2, 3), "z_act", 1)
                        elif what == "diag":
                            kind = st[1]
                            q, k = ((gq, gk), (rq, rk))[kind]
                            pe.wait_ge(sems["unit_read"], GQ + 2) if kind == GLA else pe.wait_ge(sems["rot_ready"], 4)
                            take(0, 1, 2, 3)
                            for p, g, c in chunks():
                                r, o = slice(64 * p, 64 * p + 64), g * T + c * CH
                                e = 64 * (c % 2)
                                mm(PS[e:e + 64, M0 + p, (4 * g + c // 2) * CH:(4 * g + c // 2 + 1) * CH],
                                   k[r, o:o + CH], q[r, o:o + CH])
                            for p in range(2):
                                for g in range(2):
                                    r, o = slice(64 * p, 64 * p + 64), slice(g * T + TP, (g + 1) * T)
                                    last = mm(PS[0:TS, M0 + 2 + p, g * TS:(g + 1) * TS], k[r, o], q[r, o])
                            last.then_inc(sems["pe_diag"], 1)
                            give((0, 1, 2, 3), "diag_read", kind + 1)
                        elif what == "level":
                            l = st[1]
                            H, t = LEVELS[l], QK[l % 2]
                            b0 = 2 * (l % 2)
                            take(b0, b0 + 1)
                            pe.wait_ge(sems["qk_pool"], l + 1)
                            pe.wait_ge(sems["qk_dve"], l + 1)
                            for p, g, c in chunks():
                                r, o, e = slice(64 * p, 64 * p + 64), g * T + c * CH, 64 * (c % 2)
                                rhs = t[r, o:o + CH].rearrange("p (b x h) -> p b x h", x=2, h=H)[:, :, 1, :]
                                s = (4 * g + c // 2) * 32
                                last = mm(PS[e:e + 64, M0 + b0 + p, s:s + 32], t[r, o:o + CH], rhs)
                            if H <= TS // 2:
                                for p in range(2):
                                    for g in range(2):
                                        r, o = slice(64 * p, 64 * p + 64), slice(g * T + TP, (g + 1) * T)
                                        rhs = t[r, o].rearrange("p (b x h) -> p b x h", x=2, h=H)[:, :, 1, :]
                                        last = mm(PS[0:TS, M0 + b0 + p, 256 + 16 * g:272 + 16 * g], t[r, o], rhs)
                            last.then_inc(sems["pe_lev"], 1)
                            give((b0, b0 + 1), "lev_read", l + 1)
                        elif what == "tok":
                            _, kind, kv = st
                            src = ((gv, rv), (F[0], rk))[kv == "k"][kind]
                            if kv == "v":
                                pe.wait_ge(sems["unit_read"], (GV, RV)[kind] + 2)
                            elif kind == GLA:
                                pe.wait_ge(sems["kd_ready"], 1)
                            else:
                                pe.wait_ge(sems["ret_scaled"], 2)
                            take(0, 1, 2)
                            for g in range(2):
                                for i in range(NT):
                                    nc.tensor.transpose(PS[:, M0 + g, i * P:(i + 1) * P],
                                                        src[:, g * T + i * P:g * T + (i + 1) * P], ident[:, :])
                                last = nc.tensor.transpose(PS[0:TS, M0 + 2, g * P:(g + 1) * P],
                                                           src[:, g * T + TP:(g + 1) * T], ident[:, :])
                            last.then_inc(sems["pe_tok"], 1)
                            give((0, 1, 2), "tok_read", 2 * kind + (kv == "k") + 1)
                        elif what == "kv":
                            kind = st[1]
                            take(0, 1, 2)
                            pe.wait_ge(sems["tok_read"], 2 * kind + 2)
                            for c in range(NC):
                                for g in range(2):
                                    for p in range(2):
                                        e, f = slice(64 * (c % 2), 64 * (c % 2) + 64), g * P + 64 * p
                                        o = (2 * (c // 2) + g) * HD
                                        mm(PS[64 * p:64 * p + 64, M0 + c % 2, o:o + HD], ktok[e, c // 2, f:f + HD],
                                           vtok[e, c // 2, f:f + HD])
                            for g in range(2):
                                for p in range(2):
                                    f = g * P + 64 * p
                                    last = mm(PS[64 * p:64 * p + 64, M0 + 2, g * HD:(g + 1) * HD],
                                              ktok[0:TS, NT, f:f + HD], vtok[0:TS, NT, f:f + HD])
                            last.then_inc(sems["pe_kv"], 1)
                            give((0, 1), "state_ready", 2 * NC * (kind + 1))
                            give((2,), "state_s_ready", 2 * (kind + 1))
                        elif what == "out":
                            kind = st[1]
                            qe = (qe_g, rq)[kind]
                            take(0, 1, 2, 3)
                            pe.wait_ge(sems["lev_read"], len(LEVELS))
                            pe.wait_ge(sems["state_ready"], 2 * NC * (kind + 1))
                            pe.wait_ge(sems["qe_dve"], 1) if kind == GLA else pe.wait_ge(sems["diag_read"], 2)
                            for p, g, c in chunks():
                                e, f = slice(64 * (c % 2), 64 * (c % 2) + 64), g * P + 64 * p
                                o = (2 * (c // 2) + g) * HD
                                mm(PS[e, M0 + p, o:o + HD], Pm[e, 8 * p + 4 * g + c // 2, :], vtok[e, c // 2, f:f + HD])
                            for p, g, c in chunks():
                                e, r = slice(64 * (c % 2), 64 * (c % 2) + 64), slice(64 * p, 64 * p + 64)
                                o = (2 * (c // 2) + g) * HD
                                last = mm(PS[e, M0 + 2 + p, o:o + HD], qe[r, g * T + c * CH:g * T + (c + 1) * CH], S[r, g, c, :])
                            last.then_inc(sems["pe_out"], 1)
                            give((0, 1), "out_act", kind + 1)
                            give((2, 3), "out_dve", 2 * (kind + 1))
                        elif what == "out_s":
                            kind = st[1]
                            qe = (qe_g, rq)[kind]
                            take(0, 1, 2)
                            for p in range(2):
                                for g in range(2):
                                    r, f = slice(64 * p, 64 * p + 64), g * P + 64 * p
                                    mm(PS[0:TS, M0, (2 * g + p) * HD:(2 * g + p + 1) * HD], Ps[:, 2 * p + g, :],
                                       vtok[0:TS, NT, f:f + HD])
                            pe.wait_ge(sems["state_in"], 32 * (kind + 1))
                            for p in range(2):
                                for g in range(2):
                                    r = slice(64 * p, 64 * p + 64)
                                    last = mm(PS[0:TS, M0 + 1 + p, g * HD:(g + 1) * HD], qe[r, g * T + TP:(g + 1) * T],
                                              Ss[r, g, 0, :])
                            last.then_inc(sems["pe_out_s"], 1)
                            give((0,), "outs_act", kind + 1)
                            give((1, 2), "outs_dve", 2 * (kind + 1))
                        elif what == "back":
                            kind = st[1]
                            take(0, 1, 2)
                            pe.wait_ge(sems["gn_done"], kind + 1)
                            for g in range(2):
                                for i in range(NT):
                                    o = (2 * i + g) * P
                                    nc.tensor.transpose(PS[:, M0 + g, i * P:(i + 1) * P], O[:, o:o + P], ident[:, :])
                                o = (2 * NT + g) * P
                                last = nc.tensor.transpose(PS[:, M0 + 2, g * TS:(g + 1) * TS], O[0:TS, o:o + P],
                                                           ident[0:TS, 0:TS])
                            last.then_inc(sems["pe_back"], 1)
                            give((0, 1, 2), "back_read", 2 * (kind + 1))
                        elif what == "heads":
                            u = st[1]
                            q, k, v = qkv[u % 2]
                            take(0, 1, 2, 3)
                            pe.wait_ge(sems["unit_read"], AQ + 3 * u + 3)
                            pe.wait_ge(sems[f"cache_in{u % 2}"], 32 * (u // 2 + 1))
                            for src, b, o in ((v, 0, 0), (k, 1, P)):
                                for i in range(NT):
                                    nc.tensor.transpose(PS[:, M0 + b, i * P:(i + 1) * P], src[:, i * P:(i + 1) * P], ident[:, :])
                                nc.tensor.transpose(PS[0:TS, M0 + 2, o:o + P], src[:, TP:T], ident[:, :])
                            for j in range(NT):
                                last = nc.tensor.transpose(PS[:, M0 + 3, j * P:(j + 1) * P], ckb[u % 2][:, j, :], ident[:, :])
                            last.then_inc(sems["pe_heads"], 1)
                            give((0, 1, 2), "heads_act", u + 1)
                            give((3,), "heads_dve", u + 1)
                        elif what == "score":
                            _, u, p = st
                            q, k, _ = qkv[u % 2]
                            n, r = 2 * u + p, slice(64 * p, 64 * p + 64)
                            take(0, 1, 2)
                            for i, b, c in SCORE:
                                w = (i + 1) * P
                                last = mm(PS[:, M0 + b, c:c + w], q[r, i * P:(i + 1) * P], k[r, 0:w])
                            last.then_inc(sems["pe_score"], 1)
                            for b, done in ((0, 1), (1, 3), (2, 4)):
                                give((b,), "score_dve", 4 * n + done)
                        elif what == "score_s":
                            u = st[1]
                            q, k, _ = qkv[u % 2]
                            take(3)
                            pe.wait_ge(sems["heads_dve"], u + 1)
                            for p in range(2):
                                r, e = slice(64 * p, 64 * p + 64), slice(TS * p, TS * p + TS)
                                mm(PS[e, M0 + 3, :], q[r, TP:T], kct[r, :])
                            for p in range(2):
                                r, e = slice(64 * p, 64 * p + 64), slice(64 + TS * p, 64 + TS * p + TS)
                                last = mm(PS[e, M0 + 3, 0:TS], q[r, TP:T], k[r, TP:T])
                            last.then_inc(sems["pe_score_s"], 1)
                            give((3,), "score_s_dve", 2 * u + 1)
                        elif what == "turn":
                            _, u, p = st
                            n = 2 * u + p
                            take(0, 1, 2)
                            pe.wait_ge(sems["norm_done"], n + 1)
                            for j in range(NT):
                                for i in range(j, NT):
                                    b = (0, 1, 2, 1)[j]
                                    c = T_OFF[j] - TURN_COLS[b][0] + (i - j) * P
                                    last = nc.tensor.transpose(PS[:, M0 + b, c:c + P],
                                                               Pr[p][:, P_OFF[i] + j * P:P_OFF[i] + (j + 1) * P], ident[:, :])
                            last.then_inc(sems["pe_turn"], 1)
                            for b in range(3):
                                give((b,), "turned", 3 * n + b + 1)
                        elif what == "turn_s":
                            u = st[1]
                            take(3)
                            pe.wait_ge(sems["norm_s"], u + 1)
                            for j in range(NT):
                                nc.tensor.transpose(PS[:, M0 + 3, j * 64:(j + 1) * 64], Prs[:, j * P:(j + 1) * P],
                                                    ident[0:64, 0:64])
                            last = nc.tensor.transpose(PS[0:TS, M0 + 3, 256:320], Prs[:, TP:T], ident[0:64, 0:64])
                            last.then_inc(sems["pe_turn_s"], 1)
                            give((3,), "turned_s", u + 1)
                        elif what == "pv":
                            u = st[1]
                            take(0)
                            pe.wait_ge(sems["turned"], 3 * (2 * u + 2))
                            pe.wait_ge(sems["heads_act"], u + 1)
                            for j in range(NT):
                                for p in range(2):
                                    r = slice(64 * p, 64 * p + 64)
                                    last = mm(PS[r, M0, j * P:TP], vtk[u % 2][:, j, r],
                                              PT[p][:, T_OFF[j]:T_OFF[j] + TP - j * P], j == 0, j == NT - 1)
                            last.then_inc(sems["pe_pv"], 1)
                            give((0,), "pv_dve", u + 1)
                        elif what == "pv_s":
                            u = st[1]
                            take(3)
                            pe.wait_ge(sems["turned_s"], u + 1)
                            for j in range(NT):
                                for p in range(2):
                                    r = slice(64 * p, 64 * p + 64)
                                    mm(PS[r, M0 + 3, 0:TS], cvb[u % 2][:, j, r], PTs[:, j, TS * p:TS * p + TS], j == 0, False)
                            for p in range(2):
                                r = slice(64 * p, 64 * p + 64)
                                last = mm(PS[r, M0 + 3, 0:TS], vtk[u % 2][0:TS, NT, r], PTs[0:TS, NT, TS * p:TS * p + TS],
                                          False, True)
                            last.then_inc(sems["pe_pv_s"], 1)
                            give((3,), "pvs_dve", u + 1)

                    begin(0)
                    begin(1)
                    for kc in range(KC):
                        pe.wait_ge(sems["x_lo"], kc + 1)
                        for n in range(2):
                            products(n, (xhi, xlo), (kc,), kc == 0, kc == KC - 1)
                    all_kc = tuple(range(KC))
                    for n, half in SLOTS:
                        for st in PE_STEPS.get((n, half), []):
                            stage(st)
                        if half == 0:
                            begin(n)
                        products(n, (xhi, xlo), all_kc, parts=(half,))

                    def cat_ready(kc):
                        if kc < 4:
                            pe.wait_ge(sems["cat_lo"], kc + 1)
                        else:
                            pe.wait_ge(sems["pvs_dve"], kc - 3)

                    first, later = (0, 1, 4, 5, 6), (2, 7, 3)
                    begin(N_IN)
                    products(N_IN, (zhi, zlo), first, last=False, ready=cat_ready)
                    stage(("pv_s", 3))
                    begin(N_IN + 1)
                    products(N_IN + 1, (zhi, zlo), first, last=False)
                    products(N_IN, (zhi, zlo), later, first=False, ready=cat_ready)
                    products(N_IN + 1, (zhi, zlo), later, first=False)
                    for m in range(2, KC):
                        begin(N_IN + m)
                        products(N_IN + m, (zhi, zlo), all_kc)
                    early, late = all_kc[:-1], all_kc[-1:]
                    pe.wait_ge(sems["x_lo"], 2 * KC - 1)
                    with pe.Fori(0, GROUPS) as g:
                        for k in range(N_MLP):
                            n, src = N_IN + N_OUT + k, (xhi, xlo) if k < KC else (zhi, zlo)

                            def ready(kc):
                                if k == KC:
                                    pe.wait_ge(sems["z_lo"], g * KC + (kc + 1))
                                elif kc == KC - 1:
                                    pe.wait_ge(sems["x_lo"], 2 * KC)

                            begin(n, g)
                            products(n, src, early, last=False, ready=ready if k == KC else None)
                            products(n, src, late, first=False, ready=ready if k in (0, KC) else None)

            nc.all_engine_barrier(sems_to_clear=range(layer_sems[0].num, layer_sems[-1].num + 1))

        A0, D0, E0 = 0, 2 * KC, KC
        with nc.Block() as block:
            @block.scalar
            def _(act):
                for kc in range(KC):
                    if kc >= 2:
                        act.wait_ge(once_dve, D0 + kc - 1)
                    nc.scalar.activation(sq[kc % 2][:, :], h[:, kc, :], ACT.Square).then_inc(once_act, 1)
                act.wait_ge(once_dve, D0 + KC + 1)
                nc.scalar.activation(nt[0][:, :], ssum[:, :], ACT.Ln).then_inc(once_act, 1)
                act.wait_ge(once_act, A0 + KC + 1)
                nc.scalar.activation(nt[0][:, :], nt[0][:, :], ACT.Exp, scale=-0.5).then_inc(once_act, 1)
                for i in range(NT + 1):
                    rows = P if i < NT else TS
                    act.wait_ge(once_pe, E0 + 2 + i)
                    nc.scalar.activation(yt[i][0:rows, 0:512], PS[0:rows, 2 + 2 * (i % 3), :], ACT.Copy).then_inc(once_act, 1)

            @block.vector
            def _(dve):
                n = D0
                for kc in range(KC):
                    dve.wait_ge(once_act, A0 + kc + 1)
                    if kc == 0:
                        nc.vector.tensor_copy(ssum[:, :], sq[0][:, :]).then_inc(once_dve, 1)
                    else:
                        dve.wait_ge(once_dve, n)
                        nc.vector.tensor_tensor(ssum[:, :], ssum[:, :], sq[kc % 2][:, :], ALU.add).then_inc(once_dve, 1)
                    n += 1
                dve.wait_ge(once_pe, E0 + 1)
                nc.vector.tensor_scalar(ssum[:, :].rearrange("p (a b) -> p a b", a=2), PS[:, 0:2, 0:HT], 1.0 / D, EPS,
                                        ALU.mult, ALU.add).then_inc(once_dve, 1)
                dve.wait_ge(once_dve, n + 1)
                dve.wait_ge(once_act, A0 + KC + 2)
                nc.vector.tensor_tensor(nt[1][:, :], nt[0][:, :], nt[0][:, :], ALU.mult).then_inc(once_dve, 1)
                dve.wait_ge(once_dve, n + 2)
                nc.vector.tensor_tensor(nt[1][:, :], nt[1][:, :], ssum[:, :], ALU.mult).then_inc(once_dve, 1)
                dve.wait_ge(once_dve, n + 3)
                nc.vector.tensor_scalar(nt[1][:, :], nt[1][:, :], -0.5, 1.5, ALU.mult, ALU.add).then_inc(once_dve, 1)
                dve.wait_ge(once_dve, n + 4)
                nc.vector.tensor_tensor(rstd[:, :], nt[0][:, :], nt[1][:, :], ALU.mult).then_inc(once_dve, 1)
                dve.wait_ge(once_dve, n + 5)
                for kc in range(KC):
                    nc.vector.scalar_tensor_tensor(h[:, kc, :], h[:, kc, :], wf_sb[:, kc:kc + 1], rstd[:, :],
                                                   ALU.mult, ALU.mult).then_inc(once_dve, 1)
                for i in range(NT + 1):
                    rows = P if i < NT else TS
                    dve.wait_ge(once_pe, E0 + 2 + i)
                    nc.vector.tensor_copy(yt[i][0:rows, 512:1024], PS[0:rows, 3 + 2 * (i % 3), :]).then_inc(once_dve, 1)

            @block.tensor
            def _(pe):
                pe.wait_ge(once_dve, D0 + KC)
                for a in range(2):
                    last = nc.tensor.matmul(PS[:, a, 0:HT], ones[:, :], ssum[:, a * HT:(a + 1) * HT])
                last.then_inc(once_pe, 1)
                scaled0 = D0 + KC + 5
                for i in range(NT + 1):
                    if i >= 3:
                        pe.wait_ge(once_act, A0 + KC + 2 + i - 2)
                        pe.wait_ge(once_dve, scaled0 + KC + i - 2)
                    rows = P if i < NT else TS
                    for kc in range(KC):
                        if i == 0:
                            pe.wait_ge(once_dve, scaled0 + kc + 1)
                        b, o = 2 + 2 * (i % 3) + kc // 4, (kc % 4) * P
                        last = nc.tensor.transpose(PS[0:rows, b, o:o + P], h[:, kc, i * P:i * P + rows], ident[:, :])
                    last.then_inc(once_pe, 1)

            @block.sync
            def _(sp):
                for i in range(NT + 1):
                    sp.wait_ge(once_act, A0 + KC + 2 + i + 1)
                    sp.wait_ge(once_dve, D0 + 2 * KC + 5 + i + 1)
                    if i < NT:
                        sp.dma_start(y_p[i * P:(i + 1) * P, :], yt[i][:, :]).then_inc(once_out, 16)
                    else:
                        sp.dma_start(y_s, yt[i][0:TS, :]).then_inc(once_out, 16)
                sp.wait_ge(once_out, 16 * (NT + 1))


def weight_units(w_in, w_out, w_up, w_down):
    qa, ka, va, ga, qb, kb, vb, gb, _low, qc, kc, vc = (0, 256, 512, 768, 1024, 1280, 1536, 1792, 2048, 2064, 2576, 3088)

    def unit(w):
        return w.reshape(KC, P, P).transpose(1, 0, 2).reshape(P, D)

    out = []
    for l in range(L):
        cols = []
        for base in (kb, qb, vb):
            cols += [base + g * P + np.arange(P) for g in range(2)]
        for base in (ka, qa):
            for x in range(2):
                cols.append(np.concatenate([base + hd * HD + x * 32 + np.arange(32) for hd in range(4)]))
        cols += [va + g * P + np.arange(P) for g in range(2)]
        for u in range(4):
            cols += [base + u * P + np.arange(P) for base in (qc, kc, vc)]
        for base in (ga, gb):
            cols += [base + g * P + np.arange(P) for g in range(2)]
        out += [unit(w_in[l][:, c]) for c in cols]
        out += [unit(w_out[l][:, m * P:(m + 1) * P]) for m in range(KC)]
        for g in range(GROUPS):
            out += [unit(w_up[l][:, (g * KC + k) * P:(g * KC + k + 1) * P]) for k in range(KC)]
            out += [unit(w_down[l][g * D:(g + 1) * D, m * P:(m + 1) * P]) for m in range(KC)]
    out.append(out[-1])
    return np.ascontiguousarray(np.stack(out))


def features(v, tiles):
    return v.reshape(tiles, P).T


def tables():
    f = np.float32
    pos = np.concatenate([np.arange(TP), PAST + np.arange(TS)]).astype(f)
    half = HD // 2
    inv = (f(ROPE_BASE) ** (-np.arange(half, dtype=f) / f(half))).astype(f)
    ang = (pos[None, :] * np.tile(inv, 4)[:, None]).astype(f)
    cos_t, sin_t = np.cos(ang.astype(np.float64)).astype(f), np.sin(ang.astype(np.float64)).astype(f)
    reset = np.ones((P, T), f)
    reset[:, ::CH] = 0
    lmask = np.zeros((P, len(LEVELS), 32), np.uint32)
    s = np.arange(P) % CH
    for n, H in enumerate(LEVELS):
        for j in range(32):
            lo = (j // H) * 2 * H
            lmask[:, n, j] = (s >= lo) & (s < lo + H)
    gamma = 1.0 - 2.0 ** (-5.0 - np.arange(4))
    t = np.arange(CH)
    dmask = np.zeros((P, 2, 4, CH), f)
    for p in range(2):
        for g in range(2):
            dmask[:, 0, 2 * p + g, :] = s[:, None] == t[None, :]
            d = t[None, :] - s[:, None]
            dmask[:, 1, 2 * p + g, :] = np.where(d >= 0, gamma[2 * g + p] ** np.maximum(d, 0) * HD ** -0.5, 0)
    qdec, kdec, sdec = np.zeros((P, 2, CH), f), np.zeros((P, 2, CH + TS), f), np.zeros((P, 2, 2), f)
    for g in range(2):
        for p in range(2):
            r, y = slice(64 * p, 64 * p + 64), gamma[2 * g + p]
            qdec[r, g] = y ** (t + 1)
            kdec[r, g, :CH] = y ** (CH - 1 - t) * HD ** -0.5
            kdec[r, g, CH:] = y ** (TS - 1 - t[:TS]) * HD ** -0.5
            sdec[r, g] = y ** CH, y ** TS
    return dict(cos_t=cos_t, sin_t=sin_t, reset=reset, lmask=lmask, dmask=dmask, qdec=qdec, kdec=kdec, sdec=sdec)


def kernel(x_prompt, x_sample, state_ret, state_gla, cache_attn_k, cache_attn_v, norm1_w, norm2_w, final_norm_w,
           w_in, w_gla_a2, b_gla_a, ret_gn_w, gla_norm_w, rel_bias, w_out, w_up, w_down):
    import concourse.bacc as _bacc
    from concourse.bass_utils import run_bass_kernel_spmd as _run

    f = np.float32
    (x_prompt, x_sample, state_ret, state_gla, cache_attn_k, cache_attn_v, norm1_w, norm2_w, final_norm_w,
     w_in, w_gla_a2, b_gla_a, ret_gn_w, gla_norm_w, rel_bias, w_out, w_up, w_down) = (
        np.asarray(v) for v in (x_prompt, x_sample, state_ret, state_gla, cache_attn_k, cache_attn_v, norm1_w, norm2_w,
                                final_norm_w, w_in, w_gla_a2, b_gla_a, ret_gn_w, gla_norm_w, rel_bias, w_out, w_up, w_down))
    a2 = np.zeros((L, P, 256), f)
    for j in range(4):
        a2[:, 32 * j:32 * j + 16] = w_gla_a2
    small = np.zeros((L, P, NSM), f)
    for l in range(L):
        small[l] = np.concatenate([features(norm1_w[l], KC), features(norm2_w[l], KC), features(b_gla_a[l], 2),
                                   features(ret_gn_w[l], 2), features(gla_norm_w[l], 2), np.zeros((P, 2), f)], axis=1)
    p_, m_ = np.arange(P)[:, None], np.arange(TP)[None, :]
    c_ = m_ - (TP - P)
    bias = rel_bias[:, :, np.clip(p_ - c_, -(CH - 1), 256) + CH - 1]
    bias = np.where((p_ < CH) & (c_ >= CH), f(NEG), bias)
    q_, j_ = np.arange(TS)[:, None], np.arange(T)[None, :]
    bs = rel_bias[:, :, np.clip(TP + q_ - j_, -(CH - 1), 256) + CH - 1]
    bias_s = bs.reshape(L, 4, 2 * TS, T)

    named = dict(
        x=np.concatenate([x_prompt.reshape(TP, D), x_sample.reshape(TS, D)]),
        wu=weight_units(w_in, w_out, w_up, w_down),
        w_low=w_in[:, :, 2048:2064].reshape(L, KC, P, 16).transpose(0, 2, 1, 3),
        a2=a2, small=small, wf=features(final_norm_w, KC), bias=bias, bias_s=bias_s,
        st_ret=state_ret.reshape(L, 2, P, HD), st_gla=state_gla.reshape(L, 2, P, HD),
        ck=cache_attn_k.reshape(L, TP, 512), cv=cache_attn_v.reshape(L, TP, 512), **tables())
    outs = [("y_p", (TP, D), (1, TP, D)), ("y_s", (TS, D), (1, TS, D)),
            ("ret_p", (L, 2, P, HD), (L, 1, 4, HD, HD)), ("gla_p", (L, 2, P, HD), (L, 1, 4, HD, HD)),
            ("k_p", (L, TP, 512), (L, 1, TP, 8, HD)), ("v_p", (L, TP, 512), (L, 1, TP, 8, HD)),
            ("ret_s", (L, 2, P, HD), (L, 1, 4, HD, HD)), ("gla_s", (L, 2, P, HD), (L, 1, 4, HD, HD)),
            ("k_s", (L, TS, 512), (L, 1, TS, 8, HD)), ("v_s", (L, TS, 512), (L, 1, TS, 8, HD))]
    nc = _bacc.Bacc("TRN2", target_bir_lowering=False, num_devices=1)
    arrays, args = {}, {}
    for name, a in named.items():
        a = np.ascontiguousarray(a)
        arrays[f"in_{name}"] = a
        args[name] = nc.dram_tensor(f"in_{name}", a.shape, mybir.dt.from_np(a.dtype), kind="ExternalInput").ap()
    for name, shape, _ in outs:
        args[name] = nc.dram_tensor(f"out_{name}", shape, F32, kind="ExternalOutput").ap()
    hybrid_encoder(nc, **args)
    r = _run(nc, [arrays], core_ids=[0])
    return tuple(r.results[0][f"out_{name}"].reshape(shape) for name, _, shape in outs)
```

```python
from contextlib import ExitStack

import numpy as np

import concourse.bass as bass
from concourse import mybir

P = 128
D = 1024
KC = D // P
TP, TS = 512, 32
T = TP + TS
HT = T // 2
L = 2
HD = 64
CH = 64
NC = TP // CH
NT = TP // P
FF = 4 * D
GROUPS = FF // D
LEVELS = [32, 16, 8, 4, 2, 1]
EPS = 1e-6
PRE = 2
RAW, SPL = 4, 2
N_IN, N_OUT = 28, KC
N_MLP = 2 * KC
UNITS = N_IN + N_OUT + GROUPS * N_MLP
PW = 2 * T
NEG = -1e30
M0 = 4
NSM = 24
ROPE_BASE, PAST = 10000.0, 1024

F32, F32R, U32 = mybir.dt.float32, mybir.dt.float32r, mybir.dt.uint32
ALU, ACT = mybir.AluOpType, mybir.ActivationFunctionType
AX_X = mybir.AxisListType.X
RADD = bass.bass_isa.ReduceOp.add

GK, GQ, GV, RK, RQ, RV, AQ, GATE = 0, 2, 4, 6, 8, 10, 12, 24
GLA, RET = 0, 1
TOK = [(GLA, "v"), (GLA, "k"), (RET, "k"), (RET, "v")]
PE_STEPS = {
    (2, 0): [("rms",), ("low",)],
    (3, 0): [("z", 0)], (3, 1): [("z", 1)],
    (5, 0): [("diag", GLA)],
    (5, 1): [("level", 0)], (6, 0): [("level", 1)], (6, 1): [("level", 2)],
    (7, 0): [("level", 3)], (7, 1): [("level", 4)], (8, 0): [("level", 5)],
    (8, 1): [("tok", GLA, "v")], (9, 0): [("tok", GLA, "k")], (9, 1): [("kv", GLA)],
    (10, 1): [("out", GLA)], (11, 0): [("out_s", GLA)],
    (11, 1): [("diag", RET)],
    (12, 0): [("tok", RET, "k")], (12, 1): [("tok", RET, "v")], (13, 0): [("kv", RET)],
    (13, 1): [("back", GLA)],
    (14, 0): [("out", RET)], (14, 1): [("out_s", RET)], (15, 1): [("back", RET)],
}
for _u in range(4):
    _b = 16 + 3 * _u
    PE_STEPS[(_b, 0)] = [("pv_s", _u - 1)] * (_u > 0) + [("score", _u, 0)]
    PE_STEPS[(_b, 1)] = [("heads", _u)]
    PE_STEPS[(_b + 1, 0)] = [("score", _u, 1), ("score_s", _u)]
    PE_STEPS[(_b + 1, 1)] = [("turn", _u, 0)]
    PE_STEPS[(_b + 2, 0)] = [("turn", _u, 1)]
    PE_STEPS[(_b + 2, 1)] = [("pv", _u), ("turn_s", _u)]
MID = [("back", GLA), ("back", RET), ("turn", 3, 1)]
DVE_STEPS, ACT_STEPS = dict(PE_STEPS), dict(PE_STEPS)
for _steps in (DVE_STEPS, ACT_STEPS):
    _steps[(4, 1)] = [("cum",)]
    _steps[(12, 0)] = _steps[(12, 0)] + [("gn", GLA)]
    _steps[(15, 0)] = [("gn", RET)]
GN_PARTS = [(0, 8), (8, 20)]
ROTARY = {(8, 0): (RK, 0), (8, 1): (RK, 1), (10, 0): (RQ, 0), (10, 1): (RQ, 1)}
for _u in range(4):
    _b = 16 + 3 * _u
    DVE_STEPS[(_b + 1, 0)] = [("norm", _u, 0), ("score", _u, 1)]
    DVE_STEPS[(_b + 1, 1)] = [("score_s", _u), ("norm", _u, 1)]
    DVE_STEPS[(_b + 2, 0)] = [("norm_s", _u)]
    DVE_STEPS[(_b + 2, 1)] = [("pv", _u)]
    ACT_STEPS[(_b + 1, 0)] = [("score", _u, 1)]
    ACT_STEPS[(_b, 0)] = [("pv_s", _u - 1)] * (_u > 0) + [("parts", _u, 1), ("score", _u, 0)]
    DVE_STEPS[(_b, 0)] = PE_STEPS[(_b, 0)] + [("parts", _u, 1)]
    ACT_STEPS[(_b + 1, 1)] = [("turn", _u, 0), ("score_s", _u)]
for _steps in (DVE_STEPS, ACT_STEPS):
    for _u in range(4):
        _slot = (15 + 3 * _u, 0)
        _steps[_slot] = _steps[_slot] + [("parts", _u, 0)]
SLOTS = [(n, half) for n in range(2, N_IN) for half in range(2)]

P_OFF = [0, 128, 384, 768]
T_OFF = [0, 512, 1024, 896]
P_COLS = 1280


SCORE = [(3, 0, 0), (2, 1, 0), (0, 1, 384), (1, 2, 0)]
TURN_COLS = [(0, 512), (512, 1024), (1024, 1280)]


def f32(ap):
    return ap.bitcast(F32)


def bank(n):
    return M0 + 2 if n == 2 else 2 * (n % 2)


def blocks(t, c0, c1, H):
    return t[:, c0:c1].rearrange("p (b x h) -> p b x h", x=2, h=H)


def level_parts(H):
    if 2 * H > TS:
        return [(g, g * T, g * T + TP) for g in range(2)]
    return [(0, 0, PW)]


def hybrid_encoder(nc, x, wu, w_low, a2, small, wf, bias, bias_s, st_ret, st_gla, ck, cv,
                   cos_t, sin_t, reset, lmask, dmask, qdec, kdec, sdec,
                   y_p, y_s, ret_p, gla_p, k_p, v_p, ret_s, gla_s, k_s, v_s):
    ctx = ExitStack()
    with ctx:
        place = [(nc.sbuf_base + 63) // 64 * 64]

        def at(name, shape, offset, dt=F32):
            return nc.alloc_sbuf_tensor_at(name, shape, dt, offset=offset)

        def sb(name, shape, dt=F32):
            n = int(np.prod(shape[1:])) * 4
            t = at(name, shape, place[0], dt)
            place[0] += (n + 31) // 32 * 32
            return t

        raw = [sb(f"raw{i}", [P, D]) for i in range(RAW)]
        whi = [sb(f"whi{i}", [P, D], F32R) for i in range(SPL)]
        wlo = [sb(f"wlo{i}", [P, D], F32R) for i in range(SPL)]
        h = sb("h", [P, KC, T])
        xhi, xlo = sb("xhi", [P, KC, T], F32R), sb("xlo", [P, KC, T], F32R)
        zone = place[0]
        zhi, zlo = sb("zhi", [P, KC, T], F32R), sb("zlo", [P, KC, T], F32R)
        rstd = sb("rstd", [P, T])
        r2_at = place[0]
        r2 = sb("r2", [P, T])
        sq = [sb(f"sq{i}", [P, T]) for i in range(2)]
        ssum_at = place[0]
        ssum = sb("ssum", [P, T])
        nt_at = [place[0], place[0] + 4 * T]
        nt = [sb(f"nt{i}", [P, T]) for i in range(2)]
        ident, ones = sb("ident", [P, P]), sb("ones", [P, P])
        cos_sb, sin_sb = sb("cos_sb", [P, T]), sb("sin_sb", [P, T])
        reset_sb = sb("reset_sb", [P, T])
        lm_sb = sb("lm_sb", [P, 6, 32], U32)
        dm_sb = sb("dm_sb", [P, 2, 4, CH])
        qd_sb, kd_sb = sb("qd_sb", [P, 2, CH]), sb("kd_sb", [P, 2, CH + TS])
        sd_sb = sb("sd_sb", [P, 2, 2])
        low_sb = sb("low_sb", [P, KC, 32])
        a2_sb = sb("a2_sb", [P, 256])
        sm = sb("sm", [P, NSM])
        ym, yv, yl, yr, yn = (sb(n, [P, NT + 1]) for n in ("ym", "yv", "yl", "yr", "yn"))
        dec = sb("dec", [P, 2, NC + 1])
        gst = [sb(f"gst{i}", [P, 20]) for i in range(3)]
        mx, rs = sb("mx", [P, 2, 4]), sb("rs", [P, 2, 4])
        mxs, rss = sb("mxs", [64, 1]), sb("rss", [64, 1])
        qkv = [[sb(f"att_{n}{i}", [P, T]) for n in "qkv"] for i in range(2)]
        arena = place[0]
        Z = 4 * PW
        gk, gq, gv, gb = (at(n, [P, PW], zone + i * Z) for i, n in enumerate(["gk", "gq", "gv", "gb"]))
        F = [at(f"F{i}", [P, PW], zone + (4 + i) * Z) for i in range(2)]
        qe_g = at("qe_g", [P, PW], zone + 6 * Z)
        QK = [at("QK0", [P, PW], zone + 7 * Z), at("QK1", [P, PW], arena)]
        osq = at("osq", [P, 20 * HD], zone + 4 * Z)
        oT = [at(f"oT{j}", [P, T], zone + j * 4 * T) for j in range(4)]
        Qs, Kh, Kl = ([at(f"{n}{p}", [P, T], off, F32R) for p, off in enumerate(offs)] for n, offs in (
            ("Qs", (nt_at[0], r2_at)), ("Kh", (nt_at[1], zone + 10 * 4 * T)), ("Kl", (ssum_at, zone + 11 * 4 * T))))
        G = [at(f"G{j}", [P, T], zone + (KC + j) * 4 * T) for j in range(4)]
        rot = [at("rot0", [P, T], arena + Z), at("rot1", [P, T], arena + Z + 4 * T)]
        rv, rk, rq = (at(n, [P, PW], arena + (2 + i) * Z) for i, n in enumerate(["rv", "rk", "rq"]))
        o = arena + 5 * Z
        ktok, vtok = at("ktok", [P, 5, 256], o), at("vtok", [P, 5, 256], o + 5120)
        Pm = at("Pm", [P, 16, CH], o + 10240)
        Ps = at("Ps", [TS, 4, TS], o + 14336)
        S = at("S", [P, 2, NC + 1, HD], o + 14848)
        Ss = at("Ss", [P, 2, 2, HD], o + 19456)
        O = at("O", [P, 20 * HD], o + 20480)
        end1 = o + 25600
        o = arena
        ckb = [at(f"ckb{i}", [P, NT, P], o + 2048 * i) for i in range(2)]
        cvb = [at(f"cvb{i}", [P, NT, P], o + 4096 + 2048 * i) for i in range(2)]
        Bh = [at(f"Bh{i}", [P, TP], o + 8192 + 2048 * i) for i in range(2)]
        o = arena + 3 * Z
        vtk = [at(f"vtk{i}", [P, 5, P], o + 2560 * i) for i in range(2)]
        ktk = [at(f"ktk{i}", [P, 5, P], o + 5120 + 2560 * i) for i in range(2)]
        kct = at("kct", [P, TP], o + 10240)
        Pr = [at(f"Pr{i}", [P, P_COLS], o + 12288 + 5120 * i) for i in range(2)]
        PT = [at(f"PT{i}", [P, P_COLS], o + 22528 + 5120 * i) for i in range(2)]
        PTs = at("PTs", [P, 5, 64], o + 32768)
        end2 = o + 32768 + 1280
        assert max(end1, end2) <= nc.sbuf_usable_end, (end1, end2, nc.sbuf_usable_end)
        Prs = at("Prs", [64, T], end2)
        Bs = at("Bs", [64, T], zone + (2 * KC - 1) * 4 * T)
        assert end2 + 2176 <= nc.sbuf_usable_end

        PS = ctx.enter_context(nc.psum_tensor("PS", [P, 8, 512], F32))

        def halves(t):
            return t[:, :].rearrange("p (a b) -> p a b", a=2)

        sems = {}

        def sem(name):
            if name not in sems:
                sems[name] = ctx.enter_context(nc.semaphore(name))
            return sems[name]

        tables_in, small0_in, once_dve, once_pe, once_act, once_out = (
            sem(n) for n in ("tables_in", "small0_in", "once_dve", "once_pe", "once_act", "once_out"))
        first_raw = {n: sem(f"first_raw{n}") for n in range(1, RAW)}
        const_set, x_in0, x_in1, raw_in, first_split, first_rest = (
            sem(n) for n in ("const_set", "x_in0", "x_in1", "raw_in", "first_split", "first_rest"))
        wf_in, y_turned, y_squares, y_mean, y_log, y_guess, y_link, y_rstd, y_ready = (
            sem(n) for n in ("wf_in", "y_turned", "y_squares", "y_mean", "y_log", "y_guess", "y_link", "y_rstd", "y_ready"))
        names = [
            "small_in", "state_in", "bias_in0", "bias_in1", "cache_in0", "cache_in1", "bias_s_in",
            "x_hi", "x_lo", "squared", "sq_used", "ss_ready", "ms_ready", "low_scaled", "ss_all", "newton_act", "rstd_ready",
            "w_in0", "w_in1", "w_in2", "w_in3", "w_hi", "w_lo", "unit_done", "unit_read",
            "pe_low", "low_read", "pe_rms", "pe_z", "z_act", "z_min", "cum_ready",
            "r2_steps", "lev_x", "lev_f", "qk_pool", "qk_dve", "pe_lev", "lev_read",
            "pe_diag", "diag_read", "qe_act", "qe_dve", "kd_arg", "kd_act", "kd_ready", "dec_ready",
            "pe_tok", "tok_read", "pe_kv", "state_ready", "state_s_ready", "pe_out", "out_act", "out_dve",
            "pe_out_s", "outs_act", "outs_dve", "centred", "gn_var", "gn_act", "gn_done",
            "pe_back", "back_read", "rot_ready", "ret_scaled", "o_cleared", "s_cleared",
            "part_hi", "part_lo", "pe_heads", "heads_act", "heads_dve", "pe_score", "score_dve", "max_ready", "exp_done", "norm_done",
            "pe_score_s", "score_s_dve", "exp_s", "norm_s", "pe_turn", "turned", "pe_turn_s", "turned_s",
            "pe_pv", "pv_act", "pv_dve", "pe_pv_s", "pvs_act", "pvs_dve",
            "gate_act", "gate_dve", "cat_dve", "cat_hi", "cat_lo", "relu_ready", "z_hi", "z_lo", "out_dma", "stored0", "stored1", "dve_link", "act_link", "pool_link",
        ]
        for n in names:
            sem(n)
        layer_sems = [sems[n] for n in names]
        assert [s.num for s in layer_sems] == list(range(layer_sems[0].num, layer_sems[0].num + len(names)))

        def small_loads(sp, l, done):
            sp.dma_start(sm[:, :], small[l, :, :]).then_inc(done, 16)
            sp.dma_start(low_sb[:, :, 0:16], w_low[l, :, :, :]).then_inc(done, 16)
            sp.dma_start(a2_sb[:, :], a2[l, :, :]).then_inc(done, 16)

        nc.scalar.preload_act_table_set("natural_log_exp_and_others")

        xin = [at(f"xin{i}", [P, D], arena + 4096 * i) for i in range(5)]
        with nc.Block() as block:
            @block.sync
            def _(sp):
                for half, done in enumerate((x_in0, x_in1)):
                    c = slice(half * 512, (half + 1) * 512)
                    for i in range(NT):
                        sp.dma_start(xin[i][:, c], x[i * P:(i + 1) * P, c]).then_inc(done, 16)
                    sp.dma_start(xin[4][0:TS, c], x[TP:T, c]).then_inc(done, 16)
                    if half == 0:
                        sp.dma_start(raw[0][:, :], wu[0, :, :]).then_inc(raw_in, 16)
                        sp.wait_ge(const_set, 3)
                        small_loads(sp, 0, small0_in)
                sp.dma_start(raw[1][:, :], wu[1, :, :]).then_inc(first_raw[1], 16)
                for dst, src in ((cos_sb, cos_t), (sin_sb, sin_t), (reset_sb, reset), (lm_sb, lmask),
                                 (dm_sb, dmask), (qd_sb, qdec), (kd_sb, kdec), (sd_sb, sdec)):
                    sp.dma_start(dst[:], src).then_inc(tables_in, 16)
                for n in range(2, RAW):
                    sp.dma_start(raw[n][:, :], wu[n, :, :]).then_inc(first_raw[n], 16)
                sp.wait_ge(small0_in, 16 * 3)

            @block.scalar
            def _(act):
                act.wait_ge(raw_in, 16)
                nc.scalar.activation(whi[0][:, :], raw[0][:, :], ACT.Copy).then_inc(first_split, 1)
                for kc in range(1, KC, 2):
                    if kc == 3:
                        act.wait_ge(small0_in, 16 * 3)
                        act.wait_ge(once_dve, 2)
                        act.wait_ge(once_act, 2)
                        for j in range(PRE):
                            nc.scalar.activation(xhi[:, j, :], h[:, j, :], ACT.Copy, scale=sm[:, j:j + 1]) \
                                .then_inc(first_split, 1)
                    b = 2 * (kc % 4)
                    act.wait_ge(once_pe, kc + 1)
                    nc.scalar.activation(h[:, kc, 0:TP], PS[:, b, :], ACT.Copy).then_inc(once_act, 1)
                    nc.scalar.activation(h[:, kc, TP:T], PS[:, b + 1, 0:TS], ACT.Copy).then_inc(once_act, 1)

            @block.gpsimd
            def _(pool):
                nc.gpsimd.memset(ident[:, :], 0.0).then_inc(const_set, 1)
                nc.gpsimd.memset(ones[:, :], 1.0).then_inc(const_set, 1)
                nc.gpsimd.memset(low_sb[:, :, :], 0.0).then_inc(const_set, 1)
                pool.wait_ge(const_set, 3)
                nc.gpsimd.affine_select(out=ident[:, :], in_=ident[:, :], compare_op=ALU.not_equal, fill=1.0,
                                        base=0, pattern=[[-1, P]], channel_multiplier=1).then_inc(const_set, 1)

            @block.tensor
            def _(pe):
                pe.wait_ge(const_set, 4)
                pe.wait_ge(x_in0, 16 * (NT + 1))
                for kc in range(KC):
                    b = 2 * (kc % 4)
                    if kc == KC // 2:
                        pe.wait_ge(x_in1, 16 * (NT + 1))
                    if kc >= 4:
                        pe.wait_ge((once_dve, once_act)[kc % 2], 2 * ((kc - 4) // 2 + 1))
                    for i in range(NT):
                        nc.tensor.transpose(PS[:, b, i * P:(i + 1) * P], xin[i][:, kc * P:(kc + 1) * P], ident[:, :])
                    nc.tensor.transpose(PS[:, b + 1, 0:TS], xin[4][0:TS, kc * P:(kc + 1) * P],
                                        ident[0:TS, 0:TS]).then_inc(once_pe, 1)

            @block.vector
            def _(dve):
                for kc in range(0, KC, 2):
                    b = 2 * (kc % 4)
                    dve.wait_ge(once_pe, kc + 1)
                    nc.vector.tensor_copy(h[:, kc, 0:TP], PS[:, b, :]).then_inc(once_dve, 1)
                    nc.vector.tensor_copy(h[:, kc, TP:T], PS[:, b + 1, 0:TS]).then_inc(once_dve, 1)
                dve.wait_ge(small0_in, 16 * 3)
                dve.wait_ge(first_split, 1 + PRE)
                nc.vector.tensor_tensor(wlo[0][:, :], raw[0][:, :], f32(whi[0][:, :]), ALU.subtract) \
                    .then_inc(first_rest, 1)
                for j in range(PRE):
                    nc.vector.scalar_tensor_tensor(xlo[:, j, :], h[:, j, :], sm[:, j:j + 1], f32(xhi[:, j, :]),
                                                   ALU.mult, ALU.subtract).then_inc(first_rest, 1)

        with nc.Fori(0, L) as layer:
            with nc.Block() as block:
                @block.sync
                def _(sp):
                    def load(n, j):
                        if not (isinstance(n, int) and n == RAW):
                            sp.wait_ge(sems["w_lo"], n - RAW)
                        sp.dma_start(raw[j][:, :], wu[layer * UNITS + n, :, :]).then_inc(sems[f"w_in{j}"], 16)

                    def state_in(kind):
                        if kind == RET:
                            sp.wait_ge(sems["state_s_ready"], 2)
                            sp.wait_ge(sems["outs_dve"], 2)
                            sp.wait_ge(sems["out_dma"], 16 * 4)
                        src = (st_gla, st_ret)[kind]
                        for g in range(2):
                            sp.dma_start(Ss[:, g, 0, :], src[layer, g, :, :]).then_inc(sems["state_in"], 16)

                    def band_in(u):
                        if u == 0:
                            sp.wait_ge(sems["rot_ready"], 4)
                            sp.wait_ge(sems["pe_tok"], 4)
                        for p in range(2):
                            if u >= 1:
                                sp.wait_ge(sems["score_dve"], 4 * (2 * (u - 1) + p + 1))
                            sp.dma_start(Bh[p][:, :], bias[layer, 2 * u + p, :, :]).then_inc(sems[f"bias_in{p}"], 16)
                        if u >= 2:
                            sp.wait_ge(sems["pe_heads"], u - 1)
                            sp.wait_ge(sems["pe_pv_s"], u - 1)
                        cols = slice(u * P, (u + 1) * P)
                        for dst, src in ((ckb, ck), (cvb, cv)):
                            sp.dma_start(dst[u % 2][:, :, :], src[layer, :, cols].rearrange("(j p) c -> p j c", p=P)) \
                                .then_inc(sems[f"cache_in{u % 2}"], 16)
                        if u >= 1:
                            sp.wait_ge(sems["score_s_dve"], 2 * u)
                        sp.dma_start(Bs[:, :], bias_s[layer, u, :, :]).then_inc(sems["bias_s_in"], 16)

                    def states_out(kind):
                        sp.wait_ge(sems["state_ready"], 16 * (kind + 1))
                        sp.wait_ge(sems["state_s_ready"], 2 * (kind + 1))
                        dst, dst_s = ((gla_p, gla_s), (ret_p, ret_s))[kind]
                        for g in range(2):
                            sp.dma_start(dst[layer, g, :, :], S[:, g, NC, :]).then_inc(sems["out_dma"], 16)
                            sp.dma_start(dst_s[layer, g, :, :], Ss[:, g, 1, :]).then_inc(sems["out_dma"], 16)

                    def rows_out(u):
                        sp.wait_ge(sems["heads_act"], u + 1)
                        s, cols = u % 2, slice(u * P, (u + 1) * P)
                        for dst, dst_s, src in ((k_p, k_s, ktk[s]), (v_p, v_s, vtk[s])):
                            sp.dma_start(dst[layer, :, cols].rearrange("(i p) c -> p i c", p=P), src[:, 0:NT, :]) \
                                .then_inc(sems[f"stored{s}"], 16)
                            sp.dma_start(dst_s[layer, :, cols], src[0:TS, NT, :]).then_inc(sems[f"stored{s}"], 16)

                    load(RAW, 0)
                    state_in(GLA)
                    between = {11: (states_out, GLA), 12: (state_in, RET), 14: (states_out, RET), 15: (band_in, 0),
                               17: (rows_out, 0), 18: (band_in, 1), 20: (rows_out, 1), 21: (band_in, 2),
                               23: (rows_out, 2), 24: (band_in, 3), 26: (rows_out, 3)}
                    for n in range(RAW + 1, N_IN + RAW):
                        if n - RAW in between:
                            step, arg = between[n - RAW]
                            step(arg)
                        load(n, n % RAW)
                    with sp.Fori(N_IN // RAW + 1, UNITS // RAW + 1) as i:
                        for j in range(RAW):
                            load(i * RAW + j, j)
                    small_loads(sp, layer + 1, sems["small_in"])

                @block.gpsimd
                def _(pool):
                    links = [0]

                    def link(ins):
                        links[0] += 1
                        ins.then_inc(sems["pool_link"], 1)
                        pool.wait_ge(sems["pool_link"], links[0])

                    nc.gpsimd.memset(O[:, 16 * HD:], 0.0).then_inc(sems["o_cleared"], 1)
                    nc.gpsimd.memset(S[:, :, 0, :], 0.0).then_inc(sems["s_cleared"], 1)

                    def level(l):
                        H = LEVELS[l]
                        pool.wait_ge(sems["lev_f"], 2 * (l + 1))
                        if l >= 2:
                            pool.wait_ge(sems["pe_lev"], l - 1)
                        for g, c0, c1 in level_parts(H):
                            f, q, k = (blocks(t, c0, c1, H) for t in (F[l % 2], QK[l % 2], gk))
                            ins = nc.gpsimd.tensor_tensor(q[:, :, 0, :], f[:, :, 0, :], k[:, :, 0, :], ALU.mult)
                        ins.then_inc(sems["qk_pool"], 1)

                    pool.wait_ge(sems["unit_read"], 2)
                    for l in range(len(LEVELS)):
                        level(l)

                    for m in range(KC):
                        pool.wait_ge(sems["squared"], KC + m + 1)
                        if m:
                            pool.wait_ge(sems["sq_used"], m)
                            nc.gpsimd.tensor_tensor(ssum[:, :], ssum[:, :], sq[m % 2][:, :], ALU.add) \
                                .then_inc(sems["sq_used"], 1)
                        else:
                            nc.gpsimd.tensor_scalar(ssum[:, :], sq[0][:, :], 1.0, 0.0, ALU.mult, ALU.add) \
                                .then_inc(sems["sq_used"], 1)
                    pool.wait_ge(sems["sq_used"], KC)
                    nc.gpsimd.partition_all_reduce(rstd[:, :], ssum[:, :], P, RADD).then_inc(sems["ss_all"], 1)
                    with pool.Fori(0, GROUPS) as g:
                        for m in range(KC):
                            pool.wait_ge(sems["unit_read"], g * N_MLP + (N_IN + N_OUT + KC + m + 1))
                            nc.gpsimd.tensor_tensor(h[:, m, :], h[:, m, :], sq[m % 2][:, :], ALU.add) \
                                .then_inc(sems["sq_used"], 1)

                @block.scalar
                def _(act):
                    links = [0]

                    def link(ins):
                        links[0] += 1
                        ins.then_inc(sems["act_link"], 1)
                        act.wait_ge(sems["act_link"], links[0])

                    def split(n, g=0):
                        if n >= RAW:
                            act.wait_ge(sems[f"w_in{n % RAW}"], g * (16 * N_MLP // RAW) + 16 * (n // RAW))
                        else:
                            act.wait_ge(first_raw[n], 16)
                        if n >= SPL:
                            act.wait_ge(sems["unit_done"], g * N_MLP + (n - SPL + 1))
                        nc.scalar.activation(whi[n % SPL][:, :], raw[n % RAW][:, :], ACT.Copy).then_inc(sems["w_hi"], 1)

                    def xhi_tile(kc, w):
                        nc.scalar.activation(xhi[:, kc, :], h[:, kc, :], ACT.Copy, scale=sm[:, w + kc:w + kc + 1]) \
                            .then_inc(sems["x_hi"], 1)

                    def squares(kc):
                        if kc >= 2:
                            act.wait_ge(sems["ss_ready"], kc - 1)
                        nc.scalar.activation(sq[kc % 2][:, :], h[:, kc, :], ACT.Square).then_inc(sems["squared"], 1)

                    xhi_tile(PRE, 0)
                    split(1)
                    squares(0)
                    squares(1)
                    for kc in range(PRE + 1, KC):
                        xhi_tile(kc, 0)
                        squares(kc - 1)
                    squares(KC - 1)
                    split(2)

                    def stage(st):
                        what = st[0]
                        if what == "rms":
                            act.wait_ge(sems["ms_ready"], 1)
                            link(nc.scalar.activation(nt[0][:, :], ssum[:, :], ACT.Ln))
                            nc.scalar.activation(nt[0][:, :], nt[0][:, :], ACT.Exp, scale=-0.5) \
                                .then_inc(sems["newton_act"], 1)
                        elif what == "z":
                            g = st[1]
                            act.wait_ge(sems["z_min"], g + 1)
                            f = F[0][:, g * T:(g + 1) * T]
                            nc.scalar.activation(f.rearrange("p (a b) -> p a b", a=2), PS[:, M0 + 2 * g:M0 + 2 * g + 2, 0:HT],
                                                 ACT.Abs, bias=sm[:, 16 + g:17 + g]).then_inc(sems["z_act"], 1)
                            act.wait_ge(sems["z_act"], 2 * g + 1)
                            link(nc.scalar.activation(f, f, ACT.Exp, scale=-1.0))
                            nc.scalar.activation(f, f, ACT.Ln, bias=1.0).then_inc(sems["z_act"], 1)
                        elif what == "cum":
                            level_f(0)
                            level_f(1)
                            act.wait_ge(sems["cum_ready"], 2)
                            for g in range(2):
                                nc.scalar.activation(dec[:, g, 0:NC], gb[:, g * T + CH - 1:g * T + TP:CH], ACT.Exp,
                                                     scale=1.0 / 16)
                                ins = nc.scalar.activation(dec[:, g, NC:NC + 1], gb[:, (g + 1) * T - 1:(g + 1) * T],
                                                           ACT.Exp, scale=1.0 / 16)
                            ins.then_inc(sems["dec_ready"], 1)
                        elif what == "level":
                            if st[1] + 2 < len(LEVELS):
                                level_f(st[1] + 2)
                            else:
                                late_f(st[1] + 2 - len(LEVELS))
                        elif what == "tok":
                            _, kind, kv = st
                            n = TOK.index((kind, kv))
                            dst = (vtok, ktok)[kv == "k"]
                            act.wait_ge(sems["pe_tok"], n + 1)
                            for g in range(2):
                                nc.scalar.activation(dst[:, 0:NT, g * P:(g + 1) * P],
                                                     PS[:, M0 + g, :].rearrange("p (i c) -> p i c", c=P), ACT.Copy)
                            nc.scalar.activation(dst[0:TS, NT, :], PS[0:TS, M0 + 2, 0:256], ACT.Copy) \
                                .then_inc(sems["tok_read"], 1)
                        elif what == "out":
                            act.wait_ge(sems["pe_out"], st[1] + 1)
                            if st[1] == RET:
                                act.wait_ge(sems["back_read"], 2)
                            for p in range(2):
                                o_v = O[:, 0:16 * HD].rearrange("p (a b c) -> p a b c", b=2, c=HD)[:, :, p, :]
                                ins = nc.scalar.activation(o_v, PS[:, M0 + p, :].rearrange("p (a c) -> p a c", c=HD), ACT.Copy)
                            ins.then_inc(sems["out_act"], 1)
                            act.wait_ge(sems["out_dve"], 2 * (st[1] + 1))
                            if st[1] == RET:
                                act.wait_ge(sems["centred"], 1)
                            nc.scalar.activation(osq[:, 0:16 * HD], O[:, 0:16 * HD], ACT.Square).then_inc(sems["gn_act"], 1)
                        elif what == "out_s":
                            act.wait_ge(sems["o_cleared"], 1)
                            act.wait_ge(sems["pe_out_s"], st[1] + 1)
                            nc.scalar.activation(O[0:TS, 16 * HD:], PS[0:TS, M0, 0:256], ACT.Copy) \
                                .then_inc(sems["outs_act"], 1)
                            act.wait_ge(sems["outs_dve"], 2 * (st[1] + 1))
                            if st[1] == RET:
                                act.wait_ge(sems["centred"], 2)
                            nc.scalar.activation(osq[:, 16 * HD:], O[:, 16 * HD:], ACT.Square).then_inc(sems["gn_act"], 1)
                        elif what == "gn":
                            act.wait_ge(sems["gn_var"], st[1] + 1)
                            link(nc.scalar.activation(gst[1][:, :], gst[0][:, :], ACT.Ln))
                            nc.scalar.activation(gst[1][:, :], gst[1][:, :], ACT.Exp, scale=-0.5) \
                                .then_inc(sems["gn_act"], 1)
                        elif what == "back":
                            kind = st[1]
                            act.wait_ge(sems["pe_back"], kind + 1)
                            for g in range(2):
                                j = 2 * (1 - kind) + g
                                nc.scalar.activation(oT[j][:, 0:TP], PS[:, M0 + g, :], ACT.Copy)
                                ins = nc.scalar.activation(oT[j][:, TP:T], PS[:, M0 + 2, g * TS:(g + 1) * TS], ACT.Copy)
                                ins.then_inc(sems["back_read"], 1)
                        elif what == "parts":
                            _, u, p = st
                            act.wait_ge(sems["unit_read"], AQ + 3 * u + 2)
                            if u >= 1:
                                act.wait_ge(sems["pe_score"], 2 * (u - 1) + p + 1)
                            q, k, _ = qkv[u % 2]
                            r, other = slice(64 * p, 64 * p + 64), slice(64 - 64 * p, P - 64 * p)
                            nc.scalar.activation(Qs[p][r, 0:TP], q[r, 0:TP], ACT.Copy)
                            nc.scalar.activation(Kh[p][r, 0:TP], k[r, 0:TP], ACT.Copy)
                            nc.scalar.activation(Kh[p][other, 0:TP], k[r, 0:TP], ACT.Copy).then_inc(sems["part_hi"], 1)
                        elif what == "heads":
                            u = st[1]
                            act.wait_ge(sems["pe_heads"], u + 1)
                            if u >= 2:
                                act.wait_ge(sems["pe_pv_s"], u - 1)
                                act.wait_ge(sems[f"stored{u % 2}"], 64 * (u // 2))
                            if u >= 1:
                                act.wait_ge(sems["pe_score_s"], u)
                            s = u % 2
                            nc.scalar.activation(vtk[s][:, 0:NT, :], PS[:, M0, :].rearrange("p (i c) -> p i c", c=P), ACT.Copy)
                            nc.scalar.activation(vtk[s][0:TS, NT, :], PS[0:TS, M0 + 2, 0:P], ACT.Copy)
                            nc.scalar.activation(ktk[s][0:TS, NT, :], PS[0:TS, M0 + 2, P:2 * P], ACT.Copy)
                            nc.scalar.activation(ktk[s][:, 0:NT, :], PS[:, M0 + 1, :].rearrange("p (i c) -> p i c", c=P),
                                                 ACT.Copy).then_inc(sems["heads_act"], 1)
                        elif what == "score":
                            _, u, p = st
                            act.wait_ge(sems["max_ready"], 2 * u + p + 1)
                            for i in range(NT):
                                r = Pr[p][:, P_OFF[i]:P_OFF[i] + (i + 1) * P]
                                ins = nc.scalar.activation(r, r, ACT.Exp, bias=mx[:, p, i:i + 1], accum_out=rs[:, p, i:i + 1])
                            ins.then_inc(sems["exp_done"], 1)
                        elif what == "score_s":
                            act.wait_ge(sems["score_s_dve"], 2 * (st[1] + 1))
                            nc.scalar.activation(Prs[:, :], Prs[:, :], ACT.Exp, bias=mxs[:, 0:1], accum_out=rss[:, 0:1]) \
                                .then_inc(sems["exp_s"], 1)
                        elif what == "turn":
                            _, u, p = st
                            n = 2 * u + p
                            if n == 0:
                                act.wait_ge(sems["out_dma"], 16 * 8)
                            act.wait_ge(sems["pe_turn"], n + 1)
                            if u >= 1:
                                act.wait_ge(sems["pe_pv"], u)
                            for b in range(3):
                                c0, c1 = TURN_COLS[b]
                                nc.scalar.activation(PT[p][:, c0:c1], PS[:, M0 + b, 0:c1 - c0], ACT.Copy) \
                                    .then_inc(sems["turned"], 1)
                        elif what == "turn_s":
                            u = st[1]
                            act.wait_ge(sems["pe_turn_s"], u + 1)
                            nc.scalar.activation(PTs[:, 0:NT, :], PS[:, M0 + 3, 0:256].rearrange("p (j c) -> p j c", c=64), ACT.Copy)
                            nc.scalar.activation(PTs[0:TS, NT, :], PS[0:TS, M0 + 3, 256:320], ACT.Copy) \
                                .then_inc(sems["turned_s"], 1)
                        elif what == "pv":
                            u = st[1]
                            act.wait_ge(sems["pe_pv"], u + 1)
                            nc.scalar.activation(zhi[:, 4 + u, 0:TP], PS[:, M0 + 0, :], ACT.Copy).then_inc(sems["pv_act"], 1)
                        elif what == "pv_s":
                            u = st[1]
                            act.wait_ge(sems["pe_pv_s"], u + 1)
                            nc.scalar.activation(zhi[:, 4 + u, TP:T], PS[:, M0 + 3, 0:TS], ACT.Copy).then_inc(sems["pvs_act"], 1)

                    def level_f(l):
                        H = LEVELS[l]
                        act.wait_ge(sems["lev_x"], l + 1)
                        parts = level_parts(H)
                        for side, sc in ((0, -1.0 / 16), (1, 1.0 / 16)):
                            for g, c0, c1 in parts:
                                f = blocks(F[l % 2], c0, c1, H)
                                ins = nc.scalar.activation(f[:, :, side, :], f[:, :, side, :], ACT.Exp, scale=sc)
                            ins.then_inc(sems["lev_f"], 1)

                    def late_f(which):
                        if which == 0:
                            nc.scalar.activation(qe_g[:, :], gb[:, :], ACT.Exp, scale=1.0 / 16).then_inc(sems["qe_act"], 1)
                        else:
                            act.wait_ge(sems["kd_arg"], 1)
                            nc.scalar.activation(F[0][:, :], F[0][:, :], ACT.Exp, scale=1.0 / 16).then_inc(sems["kd_act"], 1)

                    def new_x(m):
                        act.wait_ge(sems["unit_read"], N_IN + m + 1)
                        xhi_tile(m, KC)
                        if m >= 2:
                            act.wait_ge(sems["sq_used"], m - 1)
                        nc.scalar.activation(sq[m % 2][:, :], h[:, m, :], ACT.Square).then_inc(sems["squared"], 1)

                    def relu(k, g):
                        n = N_IN + N_OUT + k
                        r = nt[k % 2]
                        act.wait_ge(sems["unit_done"], g * N_MLP + (n + 1))
                        if k >= 2:
                            act.wait_ge(sems["z_lo"], g * KC + (k - 1))
                        nc.scalar.activation(halves(r), PS[:, 2 * (n % 2):2 * (n % 2) + 2, 0:HT], ACT.Relu) \
                            .then_inc(sems["relu_ready"], 1)
                        act.wait_ge(sems["unit_read"], g * N_MLP + (n + 1))
                        nc.scalar.activation(zhi[:, k, :], r[:, :], ACT.Copy).then_inc(sems["z_hi"], 1)

                    def gate_log(j):
                        e = sq[j % 2]
                        act.wait_ge(sems["unit_read"], GATE + j + 1)
                        if j >= 2:
                            act.wait_ge(sems["cat_dve"], j - 1)
                        link(nc.scalar.activation(e[:, :], G[j][:, :], ACT.Abs))
                        link(nc.scalar.activation(e[:, :], e[:, :], ACT.Exp, scale=-1.0))
                        nc.scalar.activation(e[:, :], e[:, :], ACT.Ln, bias=1.0).then_inc(sems["gate_act"], 1)

                    def gate_exp(j):
                        act.wait_ge(sems["gate_dve"], 2 * j + 1)
                        nc.scalar.activation(sq[j % 2][:, :], sq[j % 2][:, :], ACT.Exp).then_inc(sems["gate_act"], 1)

                    def gate_out(j):
                        act.wait_ge(sems["cat_dve"], j + 1)
                        nc.scalar.activation(zhi[:, j, :], G[j][:, :], ACT.Copy).then_inc(sems["cat_hi"], 1)

                    for n, half in SLOTS:
                        if half == 0:
                            split(n + 1)
                        for st in ACT_STEPS.get((n, half), []):
                            stage(st)
                        if half == 0 and n > GATE + 1:
                            gate_out(n - GATE - 2)
                        if half == 0 and n > GATE:
                            gate_log(n - GATE - 1)
                        if half == 1 and n > GATE:
                            gate_exp(n - GATE - 1)
                    for m in range(KC):
                        split(N_IN + m + 1)
                        if m == 0:
                            gate_out(2)
                            gate_log(3)
                            stage(("pv_s", 3))
                            gate_exp(3)
                            gate_out(3)
                        else:
                            new_x(m - 1)
                    new_x(KC - 1)
                    with act.Fori(0, GROUPS) as g:
                        for k in range(N_MLP):
                            n = N_IN + N_OUT + k
                            split(n + 1, g)
                            if 1 <= k <= KC:
                                relu(k - 1, g)
                    act.wait_ge(sems["small_in"], 16 * 3)
                    for kc in range(PRE):
                        act.wait_ge(sems["sq_used"], KC + (GROUPS - 1) * KC + kc + 1)
                        xhi_tile(kc, 0)
                    for j in range(1, RAW):
                        act.wait_ge(sems[f"w_in{j}"], 16 * (UNITS // RAW))
                    act.wait_ge(sems["out_dma"], 16 * 8)
                    for s in range(2):
                        act.wait_ge(sems[f"stored{s}"], 64 * 2)

                @block.vector
                def _(dve):
                    links = [0]

                    def link(ins):
                        links[0] += 1
                        ins.then_inc(sems["dve_link"], 1)
                        dve.wait_ge(sems["dve_link"], links[0])

                    def rest(n, g=0):
                        dve.wait_ge(sems["w_hi"], g * N_MLP + n)
                        nc.vector.tensor_tensor(wlo[n % SPL][:, :], raw[n % RAW][:, :], f32(whi[n % SPL][:, :]),
                                                ALU.subtract).then_inc(sems["w_lo"], 1)

                    def xlo_tile(kc, w, count):
                        dve.wait_ge(sems["x_hi"], count)
                        nc.vector.scalar_tensor_tensor(xlo[:, kc, :], h[:, kc, :], sm[:, w + kc:w + kc + 1],
                                                       f32(xhi[:, kc, :]), ALU.mult, ALU.subtract) \
                            .then_inc(sems["x_lo"], 1)

                    def newton(y, v, out, t):
                        link(nc.vector.tensor_tensor(t, y, y, ALU.mult))
                        link(nc.vector.tensor_tensor(t, t, v, ALU.mult))
                        link(nc.vector.tensor_scalar(t, t, -0.5, 1.5, ALU.mult, ALU.add))
                        return nc.vector.tensor_tensor(out, y, t, ALU.mult)

                    def add_square(kc):
                        dve.wait_ge(sems["squared"], kc + 1)
                        if kc == 0:
                            nc.vector.tensor_copy(ssum[:, :], sq[0][:, :]).then_inc(sems["ss_ready"], 1)
                        else:
                            dve.wait_ge(sems["ss_ready"], kc)
                            nc.vector.tensor_tensor(ssum[:, :], ssum[:, :], sq[kc % 2][:, :], ALU.add) \
                                .then_inc(sems["ss_ready"], 1)

                    xlo_tile(PRE, 0, 1)
                    rest(1)
                    add_square(0)
                    for kc in range(PRE + 1, KC):
                        xlo_tile(kc, 0, kc + 1 - PRE)
                        add_square(kc - 2)
                    add_square(KC - 2)
                    add_square(KC - 1)
                    nc.vector.tensor_tensor(low_sb[:, :, :], low_sb[:, :, :],
                                            sm[:, 0:KC].unsqueeze(2).to_broadcast([P, KC, 32]), ALU.mult) \
                        .then_inc(sems["low_scaled"], 1)

                    def unit_out(n):
                        src = PS[:, bank(n):bank(n) + 2, 0:HT]
                        dve.wait_ge(sems["unit_done"], n + 1)
                        if n == 0:
                            dve.wait_ge(sems["rstd_ready"], 1)

                        if n == RQ:
                            dve.wait_ge(sems["rot_ready"], 2)

                        def out(dst, by):
                            return nc.vector.tensor_tensor(dst, src, by, ALU.mult)

                        if n in (GQ, GQ + 1):
                            d = gq[:, (n - GQ) * T:(n - GQ + 1) * T].rearrange("p (a b) -> p a b", a=2)
                            ins = nc.vector.scalar_tensor_tensor(d, src, HD ** -0.5, halves(rstd), ALU.mult, ALU.mult)
                        elif n in (RK, RQ):
                            if n == RK:
                                link(nc.vector.tensor_tensor(nt[0][:, :], cos_sb[:, :], rstd[:, :], ALU.mult))
                                link(nc.vector.tensor_tensor(nt[1][:, :], sin_sb[:, :], rstd[:, :], ALU.mult))
                            link(out(halves(rot[0]), halves(nt[0])))
                            ins = out(halves(rot[1]), halves(nt[1]))
                        elif n in (RK + 1, RQ + 1):
                            link(out(halves(sq[0]), halves(nt[1])))
                            ins = out(halves(sq[1]), halves(nt[0]))
                        elif n >= GATE:
                            ins = out(halves(G[n - GATE]), halves(rstd))
                        elif n >= AQ:
                            u, which = divmod(n - AQ, 3)
                            d = halves(qkv[u % 2][which])
                            if which == 0:
                                ins = nc.vector.scalar_tensor_tensor(d, src, HD ** -0.5, halves(rstd), ALU.mult, ALU.mult)
                            else:
                                ins = out(d, halves(rstd))
                        else:
                            d, first = {0: (gk, GK), 1: (gk, GK), 4: (gv, GV), 5: (gv, GV), 10: (rv, RV), 11: (rv, RV)}[n]
                            ins = out(d[:, (n - first) * T:(n - first + 1) * T].rearrange("p (a b) -> p a b", a=2),
                                      halves(rstd))
                        ins.then_inc(sems["unit_read"], 1)

                    def rotary(first, g):
                        dst = rk if first == RK else rq
                        dve.wait_ge(sems["unit_read"], first + 2)
                        c = slice(g * T, (g + 1) * T)
                        for p in range(2):
                            s32 = slice(32 * (2 * g + p), 32 * (2 * g + p) + 32)
                            nc.vector.tensor_tensor(dst[64 * p:64 * p + 32, c], rot[0][s32, :], sq[0][s32, :], ALU.subtract)
                            ins = nc.vector.tensor_tensor(dst[64 * p + 32:64 * p + 64, c], rot[1][s32, :],
                                                          sq[1][s32, :], ALU.add)
                        ins.then_inc(sems["rot_ready"], 1)

                    def square_sums(a, b):
                        return nc.vector.reduce_sum(gst[0][:, a:b], osq[:, a * HD:b * HD].rearrange("p (a c) -> p a c", c=HD),
                                                    AX_X)

                    def centre(a, b):
                        o_v = O[:, a * HD:b * HD].rearrange("p (a c) -> p a c", c=HD)
                        m = gst[2][:, a:b]
                        link(nc.vector.reduce_sum(m, o_v, AX_X))
                        link(nc.vector.tensor_scalar(m, m, 1.0 / HD, None, ALU.mult))
                        nc.vector.tensor_tensor(o_v, o_v, m.unsqueeze(2).to_broadcast([P, b - a, HD]), ALU.subtract) \
                            .then_inc(sems["centred"], 1)

                    def level_x(l):
                        H = LEVELS[l]
                        if l >= 2:
                            dve.wait_ge(sems["qk_pool"], l - 1)
                        for g, c0, c1 in level_parts(H):
                            f, b = blocks(F[l % 2], c0, c1, H), blocks(gb, c0, c1, H)
                            nb = (c1 - c0) // (2 * H)
                            ref = b[:, :, 0:1, H - 1:H].rearrange("p b x h -> p b (x h)").to_broadcast([P, nb, 2 * H])
                            ins = nc.vector.tensor_tensor(f.rearrange("p b x h -> p b (x h)"),
                                                          b.rearrange("p b x h -> p b (x h)"), ref, ALU.subtract)
                        ins.then_inc(sems["lev_x"], 1)

                    def level_q(l):
                        H = LEVELS[l]
                        dve.wait_ge(sems["lev_f"], 2 * (l + 1))
                        if l >= 2:
                            dve.wait_ge(sems["pe_lev"], l - 1)
                        for g, c0, c1 in level_parts(H):
                            f, q, k = (blocks(t, c0, c1, H) for t in (F[l % 2], QK[l % 2], gq))
                            ins = nc.vector.tensor_tensor(q[:, :, 1, :], f[:, :, 1, :], k[:, :, 1, :], ALU.mult)
                        ins.then_inc(sems["qk_dve"], 1)

                    def stage(st):
                        what = st[0]
                        if what == "rms":
                            dve.wait_ge(sems["pe_rms"], 1)
                            nc.vector.tensor_scalar(halves(ssum), PS[:, M0 + 2:M0 + 4, 0:HT], 1.0 / D, EPS,
                                                    ALU.mult, ALU.add).then_inc(sems["ms_ready"], 1)
                            rest(2)
                            dve.wait_ge(sems["ms_ready"], 1)
                            dve.wait_ge(sems["newton_act"], 1)
                            newton(nt[0][:, :], ssum[:, :], rstd[:, :], nt[1][:, :]).then_inc(sems["rstd_ready"], 1)
                            dve.wait_ge(sems["rstd_ready"], 1)
                            dve.wait_ge(sems["pe_low"], 1)
                            nc.vector.tensor_tensor(F[1][:, 0:T].rearrange("p (a b) -> p a b", a=2),
                                                    PS[:, M0:M0 + 2, 0:HT], halves(rstd), ALU.mult) \
                                .then_inc(sems["low_read"], 1)
                            unit_out(0)
                            unit_out(1)
                        elif what == "z":
                            g = st[1]
                            dve.wait_ge(sems["pe_z"], g + 1)
                            nc.vector.tensor_scalar(gb[:, g * T:(g + 1) * T].rearrange("p (a b) -> p a b", a=2),
                                                    PS[:, M0 + 2 * g:M0 + 2 * g + 2, 0:HT], sm[:, 16 + g:17 + g], 0.0,
                                                    ALU.add, ALU.min).then_inc(sems["z_min"], 1)
                        elif what == "cum":
                            dve.wait_ge(tables_in, 16 * 8)
                            dve.wait_ge(sems["z_min"], 2)
                            dve.wait_ge(sems["z_act"], 4)
                            link(nc.vector.tensor_tensor(gb[:, :], gb[:, :], F[0][:, :], ALU.subtract))
                            for g in range(2):
                                c = slice(g * T, (g + 1) * T)
                                nc.vector.tensor_tensor_scan(gb[:, c], reset_sb[:, :], gb[:, c], 0.0, ALU.mult, ALU.add) \
                                    .then_inc(sems["cum_ready"], 1)
                            dve.wait_ge(sems["cum_ready"], 2)
                            level_x(0)
                            level_x(1)
                        elif what == "diag":
                            kind = st[1]
                            if kind == GLA:
                                level_q(0)
                            dve.wait_ge(sems["pe_diag"], kind + 1)
                            for p in range(2):
                                nc.vector.tensor_tensor(
                                    Pm[:, 8 * p:8 * p + 8, :].rearrange("p (g i) c -> p g i c", g=2),
                                    PS[:, M0 + p, :].rearrange("p (g i c) -> p g i c", g=2, c=CH),
                                    dm_sb[:, kind, 2 * p:2 * p + 2, :].unsqueeze(2).to_broadcast([P, 2, NT, CH]), ALU.mult)
                                ins = nc.vector.tensor_tensor(
                                    Ps[:, 2 * p:2 * p + 2, :], PS[0:TS, M0 + 2 + p, 0:2 * TS].rearrange("p (g c) -> p g c", g=2),
                                    dm_sb[0:TS, kind, 2 * p:2 * p + 2, 0:TS], ALU.mult)
                            ins.then_inc(sems["diag_read"], 1)
                            dve.wait_ge(sems["diag_read"], kind + 1)
                            if kind == RET:
                                for t, tab, s0 in ((rk, kd_sb, CH), (rq, qd_sb, 0)):
                                    for g in range(2):
                                        c = t[:, g * T:g * T + TP].rearrange("p (n c) -> p n c", c=CH)
                                        nc.vector.tensor_tensor(c, c, tab[:, g:g + 1, 0:CH].to_broadcast([P, NC, CH]), ALU.mult)
                                        c = t[:, g * T + TP:(g + 1) * T]
                                        ins = nc.vector.tensor_tensor(c, c, tab[:, g, s0:s0 + TS], ALU.mult)
                                    ins.then_inc(sems["ret_scaled"], 1)
                        elif what == "level":
                            l = st[1]
                            H = LEVELS[l]
                            if l + 1 < len(LEVELS):
                                level_q(l + 1)
                            if l + 2 < len(LEVELS):
                                level_x(l + 2)
                            elif l + 2 == len(LEVELS):
                                dve.wait_ge(sems["qk_pool"], 5)
                                for g in range(2):
                                    b, f = (t[:, g * T:g * T + TP].rearrange("p (n c) -> p n c", c=CH) for t in (gb, F[0]))
                                    nc.vector.tensor_tensor(f, b[:, :, CH - 1:CH].to_broadcast([P, NC, CH]), b, ALU.subtract)
                                    b, f = (t[:, g * T + TP:(g + 1) * T] for t in (gb, F[0]))
                                    ins = nc.vector.tensor_tensor(f, b[:, TS - 1:TS].to_broadcast([P, TS]), b, ALU.subtract)
                                ins.then_inc(sems["kd_arg"], 1)
                            dve.wait_ge(sems["pe_lev"], l + 1)
                            b0 = 2 * (l % 2)
                            for p in range(2):
                                nb = CH // (2 * H)
                                out = Pm[:, 8 * p:8 * p + 8, :].rearrange("p s (b x h) -> p s b x h", x=2, h=H)[:, :, :, 1, :]
                                m = lm_sb[:, l:l + 1, :].to_broadcast([P, 8, 32]).rearrange("p s (b h) -> p s b h", h=H)
                                ins = nc.vector.copy_predicated(out, m, PS[:, M0 + b0 + p, 0:256]
                                                                .rearrange("p (s b h) -> p s b h", s=8, h=H))
                                if H <= TS // 2:
                                    out = Ps[:, 2 * p:2 * p + 2, :].rearrange("p s (b x h) -> p s b x h", x=2, h=H)[:, :, :, 1, :]
                                    m = lm_sb[0:TS, l:l + 1, 0:16].to_broadcast([TS, 2, 16]).rearrange("p s (b h) -> p s b h", h=H)
                                    ins = nc.vector.copy_predicated(out, m, PS[0:TS, M0 + b0 + p, 256:288]
                                                                    .rearrange("p (s b h) -> p s b h", s=2, h=H))
                            ins.then_inc(sems["lev_read"], 1)
                            dve.wait_ge(sems["lev_read"], l + 1)
                            if l + 1 == len(LEVELS):
                                dve.wait_ge(sems["qe_act"], 1)
                                nc.vector.tensor_tensor(qe_g[:, :], qe_g[:, :], gq[:, :], ALU.mult).then_inc(sems["qe_dve"], 1)
                                dve.wait_ge(sems["kd_act"], 1)
                                nc.vector.tensor_tensor(F[0][:, :], F[0][:, :], gk[:, :], ALU.mult).then_inc(sems["kd_ready"], 1)
                        elif what == "kv":
                            kind = st[1]
                            dve.wait_ge(sems["pe_kv"], kind + 1)
                            dve.wait_ge(sems["s_cleared"], 1)
                            dve.wait_ge(sems["dec_ready"], 1)
                            if kind == RET:
                                dve.wait_ge(sems["pe_out"], 1)
                                dve.wait_ge(sems["out_dma"], 16 * 4)
                            for c in range(NC):
                                for g in range(2):
                                    if c:
                                        dve.wait_ge(sems["state_ready"], 2 * NC * kind + 2 * c - 1 + g)
                                    by = dec[:, g, c:c + 1] if kind == GLA else sd_sb[:, g, 0:1]
                                    o = (2 * (c // 2) + g) * HD
                                    nc.vector.scalar_tensor_tensor(S[:, g, c + 1, :], S[:, g, c, :], by,
                                                                   PS[:, M0 + c % 2, o:o + HD], ALU.mult, ALU.add) \
                                        .then_inc(sems["state_ready"], 1)
                            dve.wait_ge(sems["state_in"], 32 * (kind + 1))
                            for g in range(2):
                                by = dec[:, g, NC:NC + 1] if kind == GLA else sd_sb[:, g, 1:2]
                                nc.vector.scalar_tensor_tensor(Ss[:, g, 1, :], Ss[:, g, 0, :], by,
                                                               PS[:, M0 + 2, g * HD:(g + 1) * HD], ALU.mult, ALU.add) \
                                    .then_inc(sems["state_s_ready"], 1)
                        elif what == "out":
                            dve.wait_ge(sems["out_act"], st[1] + 1)
                            for p in range(2):
                                o_v = O[:, 0:16 * HD].rearrange("p (a b c) -> p a b c", b=2, c=HD)[:, :, p, :]
                                nc.vector.tensor_tensor(o_v, PS[:, M0 + 2 + p, :].rearrange("p (a c) -> p a c", c=HD), o_v,
                                                        ALU.add).then_inc(sems["out_dve"], 1)
                            if st[1] == RET:
                                dve.wait_ge(sems["out_dve"], 4)
                                centre(0, 16)
                        elif what == "out_s":
                            kind = st[1]
                            dve.wait_ge(sems["outs_act"], kind + 1)
                            for p in range(2):
                                o_v = O[0:TS, 16 * HD:].rearrange("p (a b c) -> p a b c", b=2, c=HD)[:, :, p, :]
                                nc.vector.tensor_tensor(o_v, PS[0:TS, M0 + 1 + p, 0:2 * HD].rearrange("p (a c) -> p a c", c=HD),
                                                        o_v, ALU.add).then_inc(sems["outs_dve"], 1)
                            dve.wait_ge(sems["gn_act"], 3 * kind + 1)
                            link(square_sums(0, 16))
                            dve.wait_ge(sems["outs_dve"], 2 * (kind + 1))
                            if kind == RET:
                                centre(16, 20)
                        elif what == "gn":
                            kind = st[1]
                            o_v = O[:, :].rearrange("p (a c) -> p a c", c=HD)
                            dve.wait_ge(sems["gn_act"], 3 * kind + 2)
                            link(square_sums(16, 20))
                            nc.vector.tensor_scalar(gst[0][:, :], gst[0][:, :], 1.0 / HD, EPS, ALU.mult, ALU.add) \
                                .then_inc(sems["gn_var"], 1)
                            dve.wait_ge(sems["gn_var"], kind + 1)
                            dve.wait_ge(sems["gn_act"], 3 * kind + 3)
                            link(newton(gst[1][:, :], gst[0][:, :], gst[1][:, :], gst[2][:, :]))
                            for a, b in GN_PARTS:
                                nc.vector.tensor_tensor(o_v[:, a:b, :], o_v[:, a:b, :],
                                                        gst[1][:, a:b].unsqueeze(2).to_broadcast([P, b - a, HD]), ALU.mult) \
                                    .then_inc(sems["gn_done"], 1)
                        elif what == "parts":
                            _, u, p = st
                            dve.wait_ge(sems["part_hi"], 2 * u + p + 1)
                            q, k, _ = qkv[u % 2]
                            r, other = slice(64 * p, 64 * p + 64), slice(64 - 64 * p, P - 64 * p)
                            for dst, src, hi in ((Qs[p][other, 0:TP], q, Qs), (Kl[p][r, 0:TP], k, Kh),
                                                 (Kl[p][other, 0:TP], k, Kh)):
                                ins = nc.vector.tensor_tensor(dst, src[r, 0:TP], f32(hi[p][r, 0:TP]), ALU.subtract)
                            ins.then_inc(sems["part_lo"], 1)
                        elif what == "heads":
                            u = st[1]
                            dve.wait_ge(sems["pe_heads"], u + 1)
                            if u >= 1:
                                dve.wait_ge(sems["pe_score_s"], u)
                            nc.vector.tensor_copy(kct[:, :], PS[:, M0 + 3, :]).then_inc(sems["heads_dve"], 1)
                        elif what == "score":
                            _, u, p = st
                            k = 2 * u + p
                            dve.wait_ge(sems[f"bias_in{p}"], 16 * (u + 1))
                            if u >= 1:
                                dve.wait_ge(sems["pe_turn"], 2 * (u - 1) + p + 1)
                            dve.wait_ge(sems["pe_score"], k + 1)
                            for i, b, c in SCORE:
                                w = (i + 1) * P
                                nc.vector.tensor_tensor_reduce(
                                    out=Pr[p][:, P_OFF[i]:P_OFF[i] + w], in0=PS[:, M0 + b, c:c + w], in1=Bh[p][:, TP - w:TP],
                                    scale=1.0, scalar=-3e38, op0=ALU.add, op1=ALU.max, accum_out=mx[:, p, i:i + 1]) \
                                    .then_inc(sems["score_dve"], 1)
                            dve.wait_ge(sems["score_dve"], 4 * (k + 1))
                            nc.vector.tensor_scalar(mx[:, p, :], mx[:, p, :], -1.0, None, ALU.mult).then_inc(sems["max_ready"], 1)
                        elif what == "norm":
                            _, u, p = st
                            dve.wait_ge(sems["exp_done"], 2 * u + p + 1)
                            link(nc.vector.reciprocal(rs[:, p, :], rs[:, p, :]))
                            for i in range(NT):
                                r = Pr[p][:, P_OFF[i]:P_OFF[i] + (i + 1) * P]
                                ins = nc.vector.tensor_scalar(r, r, rs[:, p, i:i + 1], None, ALU.mult)
                            ins.then_inc(sems["norm_done"], 1)
                        elif what == "score_s":
                            u = st[1]
                            dve.wait_ge(sems["bias_s_in"], 16 * (u + 1))
                            if u >= 1:
                                dve.wait_ge(sems["pe_turn_s"], u)
                            dve.wait_ge(sems["pe_score_s"], u + 1)
                            link(nc.vector.tensor_tensor(Prs[:, 0:TP], PS[0:64, M0 + 3, :], Bs[:, 0:TP], ALU.add))
                            nc.vector.tensor_tensor(Prs[:, TP:T], PS[64:P, M0 + 3, 0:TS], Bs[:, TP:T], ALU.add) \
                                .then_inc(sems["score_s_dve"], 1)
                            dve.wait_ge(sems["score_s_dve"], 2 * u + 1)
                            nc.vector.tensor_reduce(mxs[:, :], Prs[:, :], AX_X, ALU.max, negate=True) \
                                .then_inc(sems["score_s_dve"], 1)
                        elif what == "norm_s":
                            dve.wait_ge(sems["exp_s"], st[1] + 1)
                            link(nc.vector.reciprocal(rss[:, :], rss[:, :]))
                            nc.vector.tensor_scalar(Prs[:, :], Prs[:, :], rss[:, 0:1], None, ALU.mult).then_inc(sems["norm_s"], 1)
                        elif what == "pv":
                            u = st[1]
                            dve.wait_ge(sems["pv_act"], u + 1)
                            nc.vector.tensor_tensor(zlo[:, 4 + u, 0:TP], PS[:, M0, :], f32(zhi[:, 4 + u, 0:TP]), ALU.subtract) \
                                .then_inc(sems["pv_dve"], 1)
                        elif what == "pv_s":
                            u = st[1]
                            dve.wait_ge(sems["pvs_act"], u + 1)
                            nc.vector.tensor_tensor(zlo[:, 4 + u, TP:T], PS[:, M0 + 3, 0:TS], f32(zhi[:, 4 + u, TP:T]),
                                                    ALU.subtract).then_inc(sems["pvs_dve"], 1)

                    def gate_min(j):
                        e = sq[j % 2]
                        dve.wait_ge(sems["gate_act"], 2 * j + 1)
                        dve.wait_ge(sems["unit_read"], GATE + j + 1)
                        nc.vector.scalar_tensor_tensor(e[:, :], G[j][:, :], 0.0, e[:, :], ALU.min, ALU.subtract) \
                            .then_inc(sems["gate_dve"], 1)
                        dve.wait_ge(sems["back_read"], 4)
                        nc.vector.scalar_tensor_tensor(G[j][:, :], G[j][:, :], sm[:, 18 + j:19 + j], oT[j][:, :],
                                                       ALU.mult, ALU.mult).then_inc(sems["gate_dve"], 1)

                    def gate_mul(j):
                        dve.wait_ge(sems["gate_act"], 2 * j + 2)
                        dve.wait_ge(sems["gate_dve"], 2 * j + 2)
                        nc.vector.tensor_tensor(G[j][:, :], G[j][:, :], sq[j % 2][:, :], ALU.mult).then_inc(sems["cat_dve"], 1)

                    def gate_rest(j):
                        dve.wait_ge(sems["cat_hi"], j + 1)
                        nc.vector.tensor_tensor(zlo[:, j, :], G[j][:, :], f32(zhi[:, j, :]), ALU.subtract) \
                            .then_inc(sems["cat_lo"], 1)

                    for n, half in SLOTS:
                        if half == 0 and n >= 3 and n != 15:
                            unit_out(n - 1)
                        rest_first = n == 14
                        if half == 0 and rest_first:
                            rest(n + 1)
                        for st in DVE_STEPS.get((n, half), []):
                            stage(st)
                        if (n, half) == (15, 0):
                            unit_out(n - 1)
                        if half == 0 and not rest_first:
                            rest(n + 1)
                        if (n, half) in ROTARY:
                            rotary(*ROTARY[(n, half)])
                        if half == 0 and n > GATE + 1:
                            gate_rest(n - GATE - 2)
                        if half == 1 and n > GATE:
                            gate_min(n - GATE - 1)
                            gate_mul(n - GATE - 1)

                    def residual(m):
                        n = N_IN + m
                        dve.wait_ge(sems["unit_done"], n + 1)
                        hv = h[:, m, :].rearrange("p (a b) -> p a b", a=2)
                        nc.vector.tensor_tensor(hv, PS[:, 2 * (n % 2):2 * (n % 2) + 2, 0:HT], hv, ALU.add) \
                            .then_inc(sems["unit_read"], 1)

                    unit_out(N_IN - 1)
                    rest(N_IN + 1)
                    gate_rest(2)
                    gate_min(3)
                    stage(("pv_s", 3))
                    gate_mul(3)
                    gate_rest(3)
                    for m in range(1, KC + 1):
                        residual(m - 1)
                        if m < KC:
                            rest(N_IN + m + 1)
                        xlo_tile(m - 1, KC, KC - PRE + m)

                    def square(k, g):
                        n = N_IN + N_OUT + k
                        r = nt[k % 2]
                        dve.wait_ge(sems["relu_ready"], g * KC + (k + 1))
                        nc.vector.scalar_tensor_tensor(halves(r), PS[:, 2 * (n % 2):2 * (n % 2) + 2, 0:HT], 0.0, halves(r),
                                                       ALU.max, ALU.mult).then_inc(sems["unit_read"], 1)
                        dve.wait_ge(sems["z_hi"], g * KC + (k + 1))
                        nc.vector.tensor_tensor(zlo[:, k, :], r[:, :], f32(zhi[:, k, :]), ALU.subtract) \
                            .then_inc(sems["z_lo"], 1)

                    def scaled(m, g):
                        n = N_IN + N_OUT + KC + m
                        dve.wait_ge(sems["unit_done"], g * N_MLP + (n + 1))
                        dve.wait_ge(sems["sq_used"], g * KC + (KC + m - 1))
                        nc.vector.tensor_tensor(halves(sq[m % 2]), PS[:, 2 * (n % 2):2 * (n % 2) + 2, 0:HT], halves(r2),
                                                ALU.mult).then_inc(sems["unit_read"], 1)

                    with dve.Fori(0, GROUPS) as g:
                        for k in range(N_MLP):
                            rest(N_IN + N_OUT + k + 1, g)
                            if 1 <= k <= KC:
                                square(k - 1, g)
                            elif k > KC:
                                scaled(k - 1 - KC, g)
                            if k == 4:
                                dve.wait_ge(sems["ss_all"], 1)
                                nc.vector.tensor_scalar(r2[:, :], rstd[:, :], 1.0 / D, EPS, ALU.mult, ALU.add) \
                                    .then_inc(sems["r2_steps"], 1)
                            if k in (5, 6):
                                c = slice((k - 5) * HT, (k - 4) * HT)
                                dve.wait_ge(sems["r2_steps"], g * 3 + (k - 4))
                                nc.vector.reciprocal(r2[:, c], r2[:, c]).then_inc(sems["r2_steps"], 1)
                        dve.wait_ge(sems["r2_steps"], g * 3 + 3)
                        scaled(KC - 1, g)
                    dve.wait_ge(sems["small_in"], 16 * 3)
                    for kc in range(PRE):
                        xlo_tile(kc, 0, 2 * KC - PRE + kc + 1)

                @block.tensor
                def _(pe):
                    freed = {}

                    def take(*banks):
                        for b in banks:
                            if b in freed:
                                pe.wait_ge(sems[freed[b][0]], freed[b][1])

                    def give(banks, name, count):
                        for b in banks:
                            freed[b] = (name, count)

                    def mm(out, lhsT, rhs, start=True, stop=True):
                        return nc.tensor.matmul(out, lhsT, rhs, start=start, stop=stop, skip_group_check=True)

                    def begin(n, g=0):
                        if n:
                            pe.wait_ge(sems["w_lo"], g * N_MLP + n)
                        if n == 2:
                            pe.wait_ge(sems["ms_ready"], 1)
                        elif n > 2:
                            pe.wait_ge(sems["unit_read"], g * N_MLP + (n - 1))

                    def products(n, src, kcs, first=True, last=True, parts=(0, 1), ready=None):
                        (hi, lo), b, s = src, bank(n), n % SPL
                        for a in parts:
                            c, o = slice(a * HT, (a + 1) * HT), PS[:, b + a, 0:HT]
                            for kc in kcs:
                                if ready is not None and a == 0:
                                    ready(kc)
                                w = slice(kc * P, (kc + 1) * P)
                                mm(o, whi[s][:, w], hi[:, kc, c], first and kc == kcs[0], False)
                                mm(o, whi[s][:, w], lo[:, kc, c], False, False)
                                ins = mm(o, wlo[s][:, w], hi[:, kc, c], False, last and kc == kcs[-1])
                        if last and parts[-1] == 1:
                            ins.then_inc(sems["unit_done"], 1)

                    def chunks(head=None):
                        for p in range(2) if head is None else (head,):
                            for g in range(2):
                                for c in range(NC):
                                    yield p, g, c

                    def stage(st, quarter=0):
                        what = st[0]
                        if what == "low":
                            pe.wait_ge(sems["low_scaled"], 1)
                            for kk in range(2):
                                for a in range(2):
                                    for j in range(4):
                                        last = mm(PS[32 * j:32 * j + 32, M0 + a, 0:HT], low_sb[:, 2 * j + kk, :],
                                                  h[:, 2 * j + kk, a * HT:(a + 1) * HT], kk == 0, kk == 1)
                            last.then_inc(sems["pe_low"], 1)
                            give((0, 1), "low_read", 1)
                        elif what == "rms":
                            pe.wait_ge(sems["ss_ready"], KC)
                            for a in range(2):
                                last = mm(PS[:, M0 + 2 + a, 0:HT], ones[:, :], ssum[:, a * HT:(a + 1) * HT])
                            last.then_inc(sems["pe_rms"], 1)
                            give((2, 3), "ms_ready", 1)
                        elif what == "z":
                            g = st[1]
                            pe.wait_ge(sems["low_read"], 1)
                            if g == 1:
                                pe.wait_ge(sems["unit_read"], 3)
                            for a in range(2):
                                last = mm(PS[:, M0 + 2 * g + a, 0:HT], a2_sb[:, g * P:(g + 1) * P], F[1][:, a * HT:(a + 1) * HT])
                            last.then_inc(sems["pe_z"], 1)
                            give((2 * g, 2 * g + 1), "z_act", 2 * g + 1)
                        elif what == "diag":
                            kind = st[1]
                            q, k = ((gq, gk), (rq, rk))[kind]
                            pe.wait_ge(sems["unit_read"], GQ + 2) if kind == GLA else pe.wait_ge(sems["rot_ready"], 4)
                            take(0, 1, 2, 3)
                            for p, g, c in chunks():
                                r, o = slice(64 * p, 64 * p + 64), g * T + c * CH
                                e = 64 * (c % 2)
                                mm(PS[e:e + 64, M0 + p, (4 * g + c // 2) * CH:(4 * g + c // 2 + 1) * CH],
                                   k[r, o:o + CH], q[r, o:o + CH])
                            for p in range(2):
                                for g in range(2):
                                    r, o = slice(64 * p, 64 * p + 64), slice(g * T + TP, (g + 1) * T)
                                    last = mm(PS[0:TS, M0 + 2 + p, g * TS:(g + 1) * TS], k[r, o], q[r, o])
                            last.then_inc(sems["pe_diag"], 1)
                            give((0, 1, 2, 3), "diag_read", kind + 1)
                        elif what == "level":
                            l, piece = st[1], quarter % 2
                            H, t = LEVELS[l], QK[l % 2]
                            b0 = 2 * (l % 2)
                            if piece == 0:
                                take(b0, b0 + 1)
                                pe.wait_ge(sems["qk_pool"], l + 1)
                                pe.wait_ge(sems["qk_dve"], l + 1)
                            for p, g, c in chunks(piece):
                                r, o, e = slice(64 * p, 64 * p + 64), g * T + c * CH, 64 * (c % 2)
                                rhs = t[r, o:o + CH].rearrange("p (b x h) -> p b x h", x=2, h=H)[:, :, 1, :]
                                s = (4 * g + c // 2) * 32
                                last = mm(PS[e:e + 64, M0 + b0 + p, s:s + 32], t[r, o:o + CH], rhs)
                            if H <= TS // 2:
                                for p in (piece,):
                                    for g in range(2):
                                        r, o = slice(64 * p, 64 * p + 64), slice(g * T + TP, (g + 1) * T)
                                        rhs = t[r, o].rearrange("p (b x h) -> p b x h", x=2, h=H)[:, :, 1, :]
                                        last = mm(PS[0:TS, M0 + b0 + p, 256 + 16 * g:272 + 16 * g], t[r, o], rhs)
                            if piece == 1:
                                last.then_inc(sems["pe_lev"], 1)
                                give((b0, b0 + 1), "lev_read", l + 1)
                        elif what == "tok":
                            _, kind, kv = st
                            src = ((gv, rv), (F[0], rk))[kv == "k"][kind]
                            if kv == "v":
                                pe.wait_ge(sems["unit_read"], (GV, RV)[kind] + 2)
                            elif kind == GLA:
                                pe.wait_ge(sems["kd_ready"], 1)
                            else:
                                pe.wait_ge(sems["ret_scaled"], 1)
                            take(0, 1, 2)
                            for g in range(2):
                                for i in range(NT):
                                    nc.tensor.transpose(PS[:, M0 + g, i * P:(i + 1) * P],
                                                        src[:, g * T + i * P:g * T + (i + 1) * P], ident[:, :])
                                last = nc.tensor.transpose(PS[0:TS, M0 + 2, g * P:(g + 1) * P],
                                                           src[:, g * T + TP:(g + 1) * T], ident[:, :])
                            last.then_inc(sems["pe_tok"], 1)
                            give((0, 1, 2), "tok_read", TOK.index((kind, kv)) + 1)
                        elif what == "kv":
                            kind = st[1]
                            take(0, 1, 2)
                            pe.wait_ge(sems["tok_read"], 2 * kind + 2)
                            for c in range(NC):
                                for g in range(2):
                                    for p in range(2):
                                        e, f = slice(64 * (c % 2), 64 * (c % 2) + 64), g * P + 64 * p
                                        o = (2 * (c // 2) + g) * HD
                                        mm(PS[64 * p:64 * p + 64, M0 + c % 2, o:o + HD], ktok[e, c // 2, f:f + HD],
                                           vtok[e, c // 2, f:f + HD])
                            for g in range(2):
                                for p in range(2):
                                    f = g * P + 64 * p
                                    last = mm(PS[64 * p:64 * p + 64, M0 + 2, g * HD:(g + 1) * HD],
                                              ktok[0:TS, NT, f:f + HD], vtok[0:TS, NT, f:f + HD])
                            last.then_inc(sems["pe_kv"], 1)
                            give((0, 1), "state_ready", 2 * NC * (kind + 1))
                            give((2,), "state_s_ready", 2 * (kind + 1))
                        elif what == "out":
                            kind = st[1]
                            qe = (qe_g, rq)[kind]
                            take(0, 1, 2, 3)
                            pe.wait_ge(sems["lev_read"], len(LEVELS))
                            pe.wait_ge(sems["state_ready"], 2 * NC * (kind + 1))
                            pe.wait_ge(sems["qe_dve"], 1) if kind == GLA else pe.wait_ge(sems["ret_scaled"], 2)
                            for p, g, c in chunks():
                                e, f = slice(64 * (c % 2), 64 * (c % 2) + 64), g * P + 64 * p
                                o = (2 * (c // 2) + g) * HD
                                mm(PS[e, M0 + p, o:o + HD], Pm[e, 8 * p + 4 * g + c // 2, :], vtok[e, c // 2, f:f + HD])
                            for p, g, c in chunks():
                                e, r = slice(64 * (c % 2), 64 * (c % 2) + 64), slice(64 * p, 64 * p + 64)
                                o = (2 * (c // 2) + g) * HD
                                last = mm(PS[e, M0 + 2 + p, o:o + HD], qe[r, g * T + c * CH:g * T + (c + 1) * CH], S[r, g, c, :])
                            last.then_inc(sems["pe_out"], 1)
                            give((0, 1), "out_act", kind + 1)
                            give((2, 3), "out_dve", 2 * (kind + 1))
                        elif what == "out_s":
                            kind = st[1]
                            qe = (qe_g, rq)[kind]
                            take(0, 1, 2)
                            for p in range(2):
                                for g in range(2):
                                    r, f = slice(64 * p, 64 * p + 64), g * P + 64 * p
                                    mm(PS[0:TS, M0, (2 * g + p) * HD:(2 * g + p + 1) * HD], Ps[:, 2 * p + g, :],
                                       vtok[0:TS, NT, f:f + HD])
                            pe.wait_ge(sems["state_in"], 32 * (kind + 1))
                            for p in range(2):
                                for g in range(2):
                                    r = slice(64 * p, 64 * p + 64)
                                    last = mm(PS[0:TS, M0 + 1 + p, g * HD:(g + 1) * HD], qe[r, g * T + TP:(g + 1) * T],
                                              Ss[r, g, 0, :])
                            last.then_inc(sems["pe_out_s"], 1)
                            give((0,), "outs_act", kind + 1)
                            give((1, 2), "outs_dve", 2 * (kind + 1))
                        elif what == "back":
                            kind = st[1]
                            take(0, 1, 2)
                            for i in range(NT + 1):
                                if i in (0, 2):
                                    pe.wait_ge(sems["gn_done"], 2 * kind + 1 + i // 2)
                                for g in range(2):
                                    o = (2 * i + g) * P
                                    if i < NT:
                                        nc.tensor.transpose(PS[:, M0 + g, i * P:(i + 1) * P], O[:, o:o + P], ident[:, :])
                                    else:
                                        last = nc.tensor.transpose(PS[:, M0 + 2, g * TS:(g + 1) * TS], O[0:TS, o:o + P],
                                                                   ident[0:TS, 0:TS])
                            last.then_inc(sems["pe_back"], 1)
                            give((0, 1, 2), "back_read", 2 * (kind + 1))
                        elif what == "heads":
                            u = st[1]
                            q, k, v = qkv[u % 2]
                            take(0, 1, 2, 3)
                            pe.wait_ge(sems["unit_read"], AQ + 3 * u + 3)
                            pe.wait_ge(sems[f"cache_in{u % 2}"], 32 * (u // 2 + 1))
                            for src, b, o in ((v, 0, 0), (k, 1, P)):
                                for i in range(NT):
                                    nc.tensor.transpose(PS[:, M0 + b, i * P:(i + 1) * P], src[:, i * P:(i + 1) * P], ident[:, :])
                                nc.tensor.transpose(PS[0:TS, M0 + 2, o:o + P], src[:, TP:T], ident[:, :])
                            for j in range(NT):
                                last = nc.tensor.transpose(PS[:, M0 + 3, j * P:(j + 1) * P], ckb[u % 2][:, j, :], ident[:, :])
                            last.then_inc(sems["pe_heads"], 1)
                            give((0, 1, 2), "heads_act", u + 1)
                            give((3,), "heads_dve", u + 1)
                        elif what == "score":
                            _, u, p = st
                            n = 2 * u + p
                            take(0, 1, 2)
                            pe.wait_ge(sems["part_lo"], n + 1)
                            for i, b, c in SCORE:
                                w, q = (i + 1) * P, Qs[p][:, i * P:(i + 1) * P]
                                mm(PS[:, M0 + b, c:c + w], q, Kh[p][:, 0:w], True, False)
                                last = mm(PS[:, M0 + b, c:c + w], q, Kl[p][:, 0:w], False, True)
                            last.then_inc(sems["pe_score"], 1)
                            for b, done in ((0, 1), (1, 3), (2, 4)):
                                give((b,), "score_dve", 4 * n + done)
                        elif what == "score_s":
                            u = st[1]
                            q, k, _ = qkv[u % 2]
                            take(3)
                            pe.wait_ge(sems["heads_dve"], u + 1)
                            for p in range(2):
                                r, e = slice(64 * p, 64 * p + 64), slice(TS * p, TS * p + TS)
                                mm(PS[e, M0 + 3, :], q[r, TP:T], kct[r, :])
                            for p in range(2):
                                r, e = slice(64 * p, 64 * p + 64), slice(64 + TS * p, 64 + TS * p + TS)
                                last = mm(PS[e, M0 + 3, 0:TS], q[r, TP:T], k[r, TP:T])
                            last.then_inc(sems["pe_score_s"], 1)
                            give((3,), "score_s_dve", 2 * u + 1)
                        elif what == "turn":
                            _, u, p = st
                            n = 2 * u + p
                            take(0, 1, 2)
                            pe.wait_ge(sems["norm_done"], n + 1)
                            for j in range(NT):
                                for i in range(j, NT):
                                    b = (0, 1, 2, 1)[j]
                                    c = T_OFF[j] - TURN_COLS[b][0] + (i - j) * P
                                    last = nc.tensor.transpose(PS[:, M0 + b, c:c + P],
                                                               Pr[p][:, P_OFF[i] + j * P:P_OFF[i] + (j + 1) * P], ident[:, :])
                            last.then_inc(sems["pe_turn"], 1)
                            for b in range(3):
                                give((b,), "turned", 3 * n + b + 1)
                        elif what == "turn_s":
                            u = st[1]
                            take(3)
                            pe.wait_ge(sems["norm_s"], u + 1)
                            for j in range(NT):
                                nc.tensor.transpose(PS[:, M0 + 3, j * 64:(j + 1) * 64], Prs[:, j * P:(j + 1) * P],
                                                    ident[0:64, 0:64])
                            last = nc.tensor.transpose(PS[0:TS, M0 + 3, 256:320], Prs[:, TP:T], ident[0:64, 0:64])
                            last.then_inc(sems["pe_turn_s"], 1)
                            give((3,), "turned_s", u + 1)
                        elif what == "pv":
                            u = st[1]
                            take(0)
                            pe.wait_ge(sems["turned"], 3 * (2 * u + 2))
                            pe.wait_ge(sems["heads_act"], u + 1)
                            for j in range(NT):
                                for p in range(2):
                                    r = slice(64 * p, 64 * p + 64)
                                    last = mm(PS[r, M0, j * P:TP], vtk[u % 2][:, j, r],
                                              PT[p][:, T_OFF[j]:T_OFF[j] + TP - j * P], j == 0, j == NT - 1)
                            last.then_inc(sems["pe_pv"], 1)
                            give((0,), "pv_dve", u + 1)
                        elif what == "pv_s":
                            u = st[1]
                            take(3)
                            pe.wait_ge(sems["turned_s"], u + 1)
                            for j in range(NT):
                                for p in range(2):
                                    r = slice(64 * p, 64 * p + 64)
                                    mm(PS[r, M0 + 3, 0:TS], cvb[u % 2][:, j, r], PTs[:, j, TS * p:TS * p + TS], j == 0, False)
                            for p in range(2):
                                r = slice(64 * p, 64 * p + 64)
                                last = mm(PS[r, M0 + 3, 0:TS], vtk[u % 2][0:TS, NT, r], PTs[0:TS, NT, TS * p:TS * p + TS],
                                          False, True)
                            last.then_inc(sems["pe_pv_s"], 1)
                            give((3,), "pvs_dve", u + 1)

                    for kc in range(PRE + 1):
                        if kc == PRE:
                            pe.wait_ge(sems["x_lo"], 1)
                        products(0, (xhi, xlo), (kc,), kc == 0, False)
                    begin(1)
                    products(1, (xhi, xlo), tuple(range(PRE + 1)), last=False)
                    for kc in range(PRE + 1, KC):
                        pe.wait_ge(sems["x_lo"], kc + 1 - PRE)
                        for n in range(2):
                            products(n, (xhi, xlo), (kc,), False, kc == KC - 1)
                    all_kc = tuple(range(KC))
                    for n, half in SLOTS:
                        for st in PE_STEPS.get((n, half), []):
                            if st not in MID:
                                stage(st)
                        if half == 0:
                            begin(n)
                        products(n, (xhi, xlo), all_kc[:4], parts=(half,), last=False)
                        for st in PE_STEPS.get((n, half), []):
                            if st[0] == "level" or st in MID:
                                stage(st, 1)
                        products(n, (xhi, xlo), all_kc[4:], parts=(half,), first=False)

                    def cat_ready(kc):
                        if kc < 4:
                            pe.wait_ge(sems["cat_lo"], kc + 1)
                        else:
                            pe.wait_ge(sems["pvs_dve"], kc - 3)

                    first, later = (0, 1, 4, 5, 6), (2, 7, 3)
                    begin(N_IN)
                    products(N_IN, (zhi, zlo), first, last=False, ready=cat_ready)
                    stage(("pv_s", 3))
                    begin(N_IN + 1)
                    products(N_IN + 1, (zhi, zlo), first, last=False)
                    products(N_IN, (zhi, zlo), later, first=False, ready=cat_ready)
                    products(N_IN + 1, (zhi, zlo), later, first=False)
                    for m in range(2, KC):
                        begin(N_IN + m)
                        products(N_IN + m, (zhi, zlo), all_kc)
                    early, late = all_kc[:-1], all_kc[-1:]
                    pe.wait_ge(sems["x_lo"], 2 * KC - PRE - 1)
                    with pe.Fori(0, GROUPS) as g:
                        for k in range(N_MLP):
                            n, src = N_IN + N_OUT + k, (xhi, xlo) if k < KC else (zhi, zlo)

                            def ready(kc):
                                if k == KC:
                                    pe.wait_ge(sems["z_lo"], g * KC + (kc + 1))
                                elif kc == KC - 1:
                                    pe.wait_ge(sems["x_lo"], 2 * KC - PRE)

                            begin(n, g)
                            products(n, src, early, last=False, ready=ready if k == KC else None)
                            products(n, src, late, first=False, ready=ready if k in (0, KC) else None)

            nc.all_engine_barrier(sems_to_clear=range(layer_sems[0].num, layer_sems[-1].num + 1))

        ysq = at("ysq", [P, D], arena)
        yt = [at(f"yt{i}", [P, D], arena + 4096 * (1 + i)) for i in range(NT + 1)]
        wf_sb = at("wf_sb", [P, D], arena + 4096 * (NT + 2))
        with nc.Block() as block:
            def rows(i):
                return P if i < NT else TS

            def banks(i):
                return 2 * (i % 4)

            @block.sync
            def _(sp):
                sp.dma_start(wf_sb[:, :], wf).then_inc(wf_in, 16)
                for i in range(NT + 1):
                    sp.wait_ge(y_ready, 2 * (i + 1))
                    dst = y_p[i * P:(i + 1) * P, :] if i < NT else y_s
                    sp.dma_start(dst, yt[i][0:rows(i), :]).then_inc(once_out, 16)
                sp.wait_ge(once_out, 16 * (NT + 1))

            @block.tensor
            def _(pe):
                for i in range(NT + 1):
                    if i >= 4:
                        pe.wait_ge(y_ready, 2 * (i - 3))
                    for kc in range(KC):
                        b, o = banks(i) + kc // 4, (kc % 4) * P
                        last = nc.tensor.transpose(PS[0:rows(i), b, o:o + P], h[:, kc, i * P:i * P + rows(i)], ident[:, :])
                    last.then_inc(y_turned, 1)

            @block.scalar
            def _(act):
                def squares(i):
                    r = rows(i)
                    act.wait_ge(y_turned, i + 1)
                    if i >= 1:
                        act.wait_ge(y_squares, i)
                    nc.scalar.activation(ysq[0:r, :].rearrange("p (a b) -> p a b", a=2), PS[0:r, banks(i):banks(i) + 2, :],
                                         ACT.Square, accum_out=ym[0:r, i:i + 1]).then_inc(y_squares, 1)

                squares(0)
                for i in range(NT + 1):
                    r = rows(i)
                    if i < NT:
                        squares(i + 1)
                    act.wait_ge(y_mean, i + 1)
                    nc.scalar.activation(yl[0:r, i:i + 1], yv[0:r, i:i + 1], ACT.Ln).then_inc(y_log, 1)
                    act.wait_ge(y_log, i + 1)
                    nc.scalar.activation(yr[0:r, i:i + 1], yl[0:r, i:i + 1], ACT.Exp, scale=-0.5).then_inc(y_guess, 1)

            @block.gpsimd
            def _(pool):
                steps = [0]

                def link(ins):
                    steps[0] += 1
                    ins.then_inc(y_link, 1)
                    pool.wait_ge(y_link, steps[0])

                def mean(i):
                    r, c = rows(i), slice(i, i + 1)
                    pool.wait_ge(y_squares, i + 1)
                    nc.gpsimd.tensor_scalar(yv[0:r, c], ym[0:r, c], 1.0 / D, EPS, ALU.mult, ALU.add).then_inc(y_mean, 1)

                mean(0)
                for i in range(NT + 1):
                    r, c = rows(i), slice(i, i + 1)
                    pool.wait_ge(y_mean, i + 1)
                    pool.wait_ge(y_guess, i + 1)
                    link(nc.gpsimd.tensor_tensor(yn[0:r, c], yr[0:r, c], yr[0:r, c], ALU.mult))
                    link(nc.gpsimd.tensor_tensor(yn[0:r, c], yn[0:r, c], yv[0:r, c], ALU.mult))
                    link(nc.gpsimd.tensor_scalar(yn[0:r, c], yn[0:r, c], -0.5, 1.5, ALU.mult, ALU.add))
                    nc.gpsimd.tensor_tensor(yn[0:r, c], yn[0:r, c], yr[0:r, c], ALU.mult).then_inc(y_rstd, 1)
                    if i < NT:
                        mean(i + 1)

            @block.vector
            def _(dve):
                dve.wait_ge(wf_in, 16)
                for i in range(NT + 1):
                    r = rows(i)
                    dve.wait_ge(y_rstd, i + 1)
                    for a in range(2):
                        o = slice(a * 512, (a + 1) * 512)
                        nc.vector.scalar_tensor_tensor(yt[i][0:r, o], PS[0:r, banks(i) + a, :], yn[0:r, i:i + 1], wf_sb[0:r, o],
                                                       ALU.mult, ALU.mult).then_inc(y_ready, 1)


def weight_units(w_in, w_out, w_up, w_down):
    qa, ka, va, ga, qb, kb, vb, gb, _low, qc, kc, vc = (0, 256, 512, 768, 1024, 1280, 1536, 1792, 2048, 2064, 2576, 3088)

    def unit(w):
        return w.reshape(KC, P, P).transpose(1, 0, 2).reshape(P, D)

    out = []
    for l in range(L):
        cols = []
        for base in (kb, qb, vb):
            cols += [base + g * P + np.arange(P) for g in range(2)]
        for base in (ka, qa):
            for x in range(2):
                cols.append(np.concatenate([base + hd * HD + x * 32 + np.arange(32) for hd in range(4)]))
        cols += [va + g * P + np.arange(P) for g in range(2)]
        for u in range(4):
            cols += [base + u * P + np.arange(P) for base in (qc, kc, vc)]
        for base in (ga, gb):
            cols += [base + g * P + np.arange(P) for g in range(2)]
        out += [unit(w_in[l][:, c]) for c in cols]
        out += [unit(w_out[l][:, m * P:(m + 1) * P]) for m in range(KC)]
        for g in range(GROUPS):
            out += [unit(w_up[l][:, (g * KC + k) * P:(g * KC + k + 1) * P]) for k in range(KC)]
            out += [unit(w_down[l][g * D:(g + 1) * D, m * P:(m + 1) * P]) for m in range(KC)]
    out += out[-1:] * RAW
    return np.ascontiguousarray(np.stack(out))


def features(v, tiles):
    return v.reshape(tiles, P).T


def once_more(a):
    return np.concatenate([a, a[-1:]])


def tables():
    f = np.float32
    pos = np.concatenate([np.arange(TP), PAST + np.arange(TS)]).astype(f)
    half = HD // 2
    inv = (f(ROPE_BASE) ** (-np.arange(half, dtype=f) / f(half))).astype(f)
    ang = (pos[None, :] * np.tile(inv, 4)[:, None]).astype(f)
    cos_t, sin_t = np.cos(ang.astype(np.float64)).astype(f), np.sin(ang.astype(np.float64)).astype(f)
    reset = np.ones((P, T), f)
    reset[:, ::CH] = 0
    lmask = np.zeros((P, len(LEVELS), 32), np.uint32)
    s = np.arange(P) % CH
    for n, H in enumerate(LEVELS):
        for j in range(32):
            lo = (j // H) * 2 * H
            lmask[:, n, j] = (s >= lo) & (s < lo + H)
    gamma = 1.0 - 2.0 ** (-5.0 - np.arange(4))
    t = np.arange(CH)
    dmask = np.zeros((P, 2, 4, CH), f)
    for p in range(2):
        for g in range(2):
            dmask[:, 0, 2 * p + g, :] = s[:, None] == t[None, :]
            d = t[None, :] - s[:, None]
            dmask[:, 1, 2 * p + g, :] = np.where(d >= 0, gamma[2 * g + p] ** np.maximum(d, 0) * HD ** -0.5, 0)
    qdec, kdec, sdec = np.zeros((P, 2, CH), f), np.zeros((P, 2, CH + TS), f), np.zeros((P, 2, 2), f)
    for g in range(2):
        for p in range(2):
            r, y = slice(64 * p, 64 * p + 64), gamma[2 * g + p]
            qdec[r, g] = y ** (t + 1)
            kdec[r, g, :CH] = y ** (CH - 1 - t) * HD ** -0.5
            kdec[r, g, CH:] = y ** (TS - 1 - t[:TS]) * HD ** -0.5
            sdec[r, g] = y ** CH, y ** TS
    return dict(cos_t=cos_t, sin_t=sin_t, reset=reset, lmask=lmask, dmask=dmask, qdec=qdec, kdec=kdec, sdec=sdec)


def kernel(x_prompt, x_sample, state_ret, state_gla, cache_attn_k, cache_attn_v, norm1_w, norm2_w, final_norm_w,
           w_in, w_gla_a2, b_gla_a, ret_gn_w, gla_norm_w, rel_bias, w_out, w_up, w_down):
    import concourse.bacc as _bacc
    from concourse.bass_utils import run_bass_kernel_spmd as _run

    f = np.float32
    (x_prompt, x_sample, state_ret, state_gla, cache_attn_k, cache_attn_v, norm1_w, norm2_w, final_norm_w,
     w_in, w_gla_a2, b_gla_a, ret_gn_w, gla_norm_w, rel_bias, w_out, w_up, w_down) = (
        np.asarray(v) for v in (x_prompt, x_sample, state_ret, state_gla, cache_attn_k, cache_attn_v, norm1_w, norm2_w,
                                final_norm_w, w_in, w_gla_a2, b_gla_a, ret_gn_w, gla_norm_w, rel_bias, w_out, w_up, w_down))
    a2 = np.zeros((L, P, 256), f)
    for j in range(4):
        a2[:, 32 * j:32 * j + 16] = w_gla_a2
    small = np.zeros((L, P, NSM), f)
    for l in range(L):
        small[l] = np.concatenate([features(norm1_w[l], KC), features(norm2_w[l], KC), features(b_gla_a[l], 2),
                                   features(ret_gn_w[l], 2), features(gla_norm_w[l], 2), np.zeros((P, 2), f)], axis=1)
    p_, m_ = np.arange(P)[:, None], np.arange(TP)[None, :]
    c_ = m_ - (TP - P)
    bias = rel_bias[:, :, np.clip(p_ - c_, -(CH - 1), 256) + CH - 1]
    bias = np.where((p_ < CH) & (c_ >= CH), f(NEG), bias)
    q_, j_ = np.arange(TS)[:, None], np.arange(T)[None, :]
    bs = rel_bias[:, :, np.clip(TP + q_ - j_, -(CH - 1), 256) + CH - 1]
    bias_s = bs.reshape(L, 4, 2 * TS, T)

    named = dict(
        x=np.concatenate([x_prompt.reshape(TP, D), x_sample.reshape(TS, D)]),
        wu=weight_units(w_in, w_out, w_up, w_down),
        w_low=once_more(w_in[:, :, 2048:2064].reshape(L, KC, P, 16).transpose(0, 2, 1, 3)),
        a2=once_more(a2), small=once_more(small), wf=np.broadcast_to(final_norm_w, (P, D)), bias=bias, bias_s=bias_s,
        st_ret=state_ret.reshape(L, 2, P, HD), st_gla=state_gla.reshape(L, 2, P, HD),
        ck=cache_attn_k.reshape(L, TP, 512), cv=cache_attn_v.reshape(L, TP, 512), **tables())
    outs = [("y_p", (TP, D), (1, TP, D)), ("y_s", (TS, D), (1, TS, D)),
            ("ret_p", (L, 2, P, HD), (L, 1, 4, HD, HD)), ("gla_p", (L, 2, P, HD), (L, 1, 4, HD, HD)),
            ("k_p", (L, TP, 512), (L, 1, TP, 8, HD)), ("v_p", (L, TP, 512), (L, 1, TP, 8, HD)),
            ("ret_s", (L, 2, P, HD), (L, 1, 4, HD, HD)), ("gla_s", (L, 2, P, HD), (L, 1, 4, HD, HD)),
            ("k_s", (L, TS, 512), (L, 1, TS, 8, HD)), ("v_s", (L, TS, 512), (L, 1, TS, 8, HD))]
    nc = _bacc.Bacc("TRN2", target_bir_lowering=False, num_devices=1)
    arrays, args = {}, {}
    for name, a in named.items():
        a = np.ascontiguousarray(a)
        arrays[f"in_{name}"] = a
        args[name] = nc.dram_tensor(f"in_{name}", a.shape, mybir.dt.from_np(a.dtype), kind="ExternalInput").ap()
    for name, shape, _ in outs:
        args[name] = nc.dram_tensor(f"out_{name}", shape, F32, kind="ExternalOutput").ap()
    hybrid_encoder(nc, **args)
    r = _run(nc, [arrays], core_ids=[0])
    return tuple(r.results[0][f"out_{name}"].reshape(shape) for name, _, shape in outs)
```
